# Optimizing a Trainium2 kernel written in Bass

```python
import jax, jax.numpy as jnp
from jax import lax
import numpy as np

D_MODEL = 1024
BATCH = 1
SEQ = 256
DEPTH = 1

CHUNK = 64
SB_HEADS = 8
SB_HEAD_DIM = 64
SB_WIDTH = SB_HEADS * SB_HEAD_DIM
Q_BLOCK = 128
S5_WIDTH = D_MODEL // 2
S5_GROUP = 16
S5_GROUPS = S5_WIDTH // S5_GROUP
S5_STATE = 64
S5_DT_MIN = 1e-3
S5_DT_MAX = 1e-1
N_EXPERTS = 32
TOP_K = 4
D_FF = D_MODEL
SWIGLU_LIMIT = 7.0
SWIGLU_ALPHA = 1.702
RMS_EPS = 1e-5
OFF_K = SB_WIDTH
OFF_V = 2 * SB_WIDTH
OFF_U = 3 * SB_WIDTH
OFF_GA = OFF_U + S5_WIDTH
OFF_GB = OFF_GA + D_MODEL
IN_WIDTH = OFF_GB + D_MODEL

kernel_name = "hybrid_stickbreak_s5_moe_block"

def rmsnorm(x, g):
    xf = x.astype(jnp.float32)
    return xf * lax.rsqrt(jnp.mean(xf * xf, axis=-1, keepdims=True) + RMS_EPS) * g.astype(jnp.float32)

def split_heads(t):
    b, l, _ = t.shape
    return t.reshape(b, l, SB_HEADS, SB_HEAD_DIM).transpose(0, 2, 1, 3)

def stick_breaking_attention(q, k, v):
    scale = SB_HEAD_DIM ** -0.5
    seq = q.shape[2]
    outs = []
    for start in range(0, seq, Q_BLOCK):
        end = start + Q_BLOCK
        qb = q[:, :, start:end]
        kb = k[:, :, :end]
        vb = v[:, :, :end]
        z = jnp.einsum('bhqd,bhkd->bhqk', qb, kb).astype(jnp.float32) * scale
        before = jnp.arange(end)[None, :] < jnp.arange(start, end)[:, None]
        log_keep = jnp.where(before, jax.nn.log_sigmoid(-z), 0.0)
        later = lax.cumsum(log_keep, axis=3, reverse=True) - log_keep
        w = jnp.where(before, jnp.exp(jax.nn.log_sigmoid(z) + later), 0.0)
        outs.append(jnp.einsum('bhqk,bhkd->bhqd', w, vb.astype(jnp.float32)))
    return jnp.concatenate(outs, axis=2)

def s5_mixer(u, lam_re, lam_im, b_re, b_im, c_re, c_im, d_skip, log_step, w_glu):
    f32 = jnp.float32
    bsz, seq, _ = u.shape
    uf = u.astype(f32).reshape(bsz, seq, S5_GROUPS, S5_GROUP)
    lam = lax.complex(lam_re.astype(f32), lam_im.astype(f32))
    step = jnp.exp(log_step.astype(f32))[:, None]
    lam_bar = jnp.exp(lam * step)
    b_mat = lax.complex(b_re.astype(f32), b_im.astype(f32))
    b_bar = ((lam_bar - 1.0) / lam)[:, :, None] * b_mat
    bu = jnp.einsum('gph,blgh->blgp', b_bar, uf)
    decay = jnp.broadcast_to(lam_bar, (1, seq, S5_GROUPS, S5_STATE))

    def combine(left, right):
        a_l, s_l = left
        a_r, s_r = right
        return a_l * a_r, a_r * s_l + s_r

    _, states = lax.associative_scan(combine, (decay, bu), axis=1)
    c_mat = lax.complex(c_re.astype(f32), c_im.astype(f32))
    y = jnp.real(jnp.einsum('ghp,blgp->blgh', c_mat, states)) + d_skip.astype(f32) * uf
    y = jax.nn.gelu(y.reshape(bsz, seq, S5_WIDTH))
    return y * jax.nn.sigmoid(y @ w_glu)

def moe_ffn(h, w_router, b_router, w_up, b_up, w_down, b_down):
    bsz, seq, d = h.shape
    t = h.reshape(bsz * seq, d)
    logits = (t @ w_router + b_router).astype(jnp.float32)
    top_val, top_idx = lax.top_k(logits, TOP_K)
    top_w = jax.nn.softmax(top_val, axis=-1)
    gates = jnp.sum(jax.nn.one_hot(top_idx, N_EXPERTS, dtype=jnp.float32) * top_w[..., None], axis=1)
    out = jnp.zeros((bsz * seq, d), jnp.float32)
    for e in range(N_EXPERTS):
        hid = t @ w_up[e] + b_up[e]
        glu = jnp.minimum(hid[:, :D_FF], SWIGLU_LIMIT)
        lin = jnp.clip(hid[:, D_FF:], -SWIGLU_LIMIT, SWIGLU_LIMIT)
        act = glu * jax.nn.sigmoid(SWIGLU_ALPHA * glu) * (lin + 1.0)
        out = out + gates[:, e:e + 1] * (act @ w_down[e] + b_down[e])
    return out.reshape(bsz, seq, d)

def setup_inputs(seed: int = 0) -> dict:
    key = jax.random.key(seed)
    ks = jax.random.split(key, 24)
    f32 = jnp.float32

    def nrm(k, shape, scale):
        return jax.random.normal(k, shape, f32) * scale

    L = DEPTH
    G, P, H = S5_GROUPS, S5_STATE, S5_GROUP
    n_idx = jnp.arange(P, dtype=f32)
    return {
        "x": nrm(ks[0], (BATCH, SEQ, D_MODEL), 1.0),
        "norm_mix": 1.0 + nrm(ks[1], (L, D_MODEL), 0.02),
        "w_in": nrm(ks[2], (L, D_MODEL, IN_WIDTH), D_MODEL ** -0.5),
        "s5_lam_re": -0.5 + nrm(ks[3], (L, G, P), 0.01),
        "s5_lam_im": jnp.pi * n_idx + nrm(ks[4], (L, G, P), 0.01),
        "s5_b_re": nrm(ks[5], (L, G, P, H), (2 * H) ** -0.5),
        "s5_b_im": nrm(ks[6], (L, G, P, H), (2 * H) ** -0.5),
        "s5_c_re": nrm(ks[7], (L, G, H, P), (2 * P) ** -0.5),
        "s5_c_im": nrm(ks[8], (L, G, H, P), (2 * P) ** -0.5),
        "s5_d": nrm(ks[9], (L, G, H), 1.0),
        "s5_log_step": jax.random.uniform(ks[10], (L, G), f32, float(np.log(S5_DT_MIN)), float(np.log(S5_DT_MAX))),
        "w_glu": nrm(ks[11], (L, S5_WIDTH, S5_WIDTH), S5_WIDTH ** -0.5),
        "w_branch_sb": nrm(ks[12], (L, SB_WIDTH, D_MODEL), SB_WIDTH ** -0.5),
        "w_branch_s5": nrm(ks[13], (L, S5_WIDTH, D_MODEL), S5_WIDTH ** -0.5),
        "w_out": nrm(ks[14], (L, D_MODEL, D_MODEL), D_MODEL ** -0.5),
        "norm_ffn": 1.0 + nrm(ks[15], (L, D_MODEL), 0.02),
        "w_router": nrm(ks[16], (L, D_MODEL, N_EXPERTS), D_MODEL ** -0.5),
        "b_router": nrm(ks[17], (L, N_EXPERTS), 0.01),
        "w_up": nrm(ks[18], (L, N_EXPERTS, D_MODEL, 2 * D_FF), D_MODEL ** -0.5),
        "b_up": nrm(ks[19], (L, N_EXPERTS, 2 * D_FF), 0.01),
        "w_down": nrm(ks[20], (L, N_EXPERTS, D_FF, D_MODEL), D_FF ** -0.5),
        "b_down": nrm(ks[21], (L, N_EXPERTS, D_MODEL), 0.01),
        "norm_final": 1.0 + nrm(ks[22], (D_MODEL,), 0.02),
    }

def reference(x, norm_mix, w_in, s5_lam_re, s5_lam_im, s5_b_re, s5_b_im, s5_c_re, s5_c_im,
              s5_d, s5_log_step, w_glu, w_branch_sb, w_branch_s5, w_out, norm_ffn,
              w_router, b_router, w_up, b_up, w_down, b_down, norm_final):
    bsz, seq, _ = x.shape
    for l in range(DEPTH):
        h = rmsnorm(x, norm_mix[l])
        proj = h @ w_in[l]
        q = split_heads(proj[..., :OFF_K])
        k = split_heads(proj[..., OFF_K:OFF_V])
        v = split_heads(proj[..., OFF_V:OFF_U])
        u = proj[..., OFF_U:OFF_GA]
        gate_sb = jax.nn.sigmoid(proj[..., OFF_GA:OFF_GB])
        gate_s5 = jax.nn.sigmoid(proj[..., OFF_GB:])
        y_sb = stick_breaking_attention(q, k, v).transpose(0, 2, 1, 3).reshape(bsz, seq, SB_WIDTH)
        y_s5 = s5_mixer(u, s5_lam_re[l], s5_lam_im[l], s5_b_re[l], s5_b_im[l], s5_c_re[l], s5_c_im[l],
                        s5_d[l], s5_log_step[l], w_glu[l])
        merged = gate_sb * (y_sb @ w_branch_sb[l]) + gate_s5 * (y_s5 @ w_branch_s5[l])
        x = x + (merged @ w_out[l]).astype(x.dtype)
        h = rmsnorm(x, norm_ffn[l])
        x = x + moe_ffn(h, w_router[l], b_router[l], w_up[l], b_up[l], w_down[l], b_down[l]).astype(x.dtype)
    return rmsnorm(x, norm_final).astype(x.dtype)


_drawn_inputs = setup_inputs


def setup_inputs(seed=0):
    import zlib

    import numpy as np

    out = dict(_drawn_inputs(seed))
    spreads = {}
    factors = {'s5_lam_re': 200.0,
     'b_up': 8.0,
     'b_down': 8.0,
     'norm_final': 22.55,
     's5_lam_im': 2.929,
     's5_b_re': 8.423,
     's5_b_im': 6.307,
     's5_c_re': 2.849,
     's5_c_im': 2.716}
    for name, (base, spread) in spreads.items():
        noise = np.random.default_rng([zlib.crc32(name.encode()), seed]).standard_normal(out[name].shape)
        drawn = base * np.exp(spread * noise) if base else spread * noise
        out[name] = __import__('jax').numpy.asarray(drawn.astype(out[name].dtype))
    for name, factor in factors.items():
        out[name] = (out[name] * factor).astype(out[name].dtype)
    return out
```

```python
from contextlib import ExitStack

import concourse.bass as bass
from concourse import mybir

F32 = mybir.dt.float32
BF16 = mybir.dt.bfloat16
I32 = mybir.dt.int32
U32 = mybir.dt.uint32
ALU = mybir.AluOpType
ACT = mybir.ActivationFunctionType
AX = mybir.AxisListType

P = 128
T = 256
NT = T // P
D = 1024
KC = D // P
HEADS, HD = 8, 64
GROUPS, GCH, NSTATE = 32, 16, 64
PAIRS = GROUPS // 2
CW = 4
E = 32
TOPK = 4
FF = 1024
SLOTS = 64
MAXR = T // SLOTS
NV = MAXR * E + 1
UPC = KC
DNC = KC // 2
RING = UPC + DNC
RW = 2 * FF
EPS = 1e-5
LIMIT, ALPHA = 7.0, 1.702
TWO_PI = 6.283185307179586
PI_A = 6.28125
PI_B = 0.0019353071693331003
PI_C = 1.02520991e-11
MAGIC = 12582912.0
GELU_C = 0.044715
GELU_S = 1.5957691216057308
NOT_ROUTED = 4096.0

GROUP_ORDER = [3, 0, 1, 2, 4, 5, 6, 7]
NHALF = 2 * len(GROUP_ORDER)
WIN_SLOTS = 4
ATT_FROM = 8
S5_FROM = 3


def s5_steps_after(n):
    return 0 if n < S5_FROM else min(PAIRS + 2, ((n - S5_FROM + 1) * 3 + 1) // 2)


def build(nc, x, norm_mix, w_in, s5_lam_re, s5_lam_im, s5_b_re, s5_b_im, s5_c_re, s5_c_im, s5_d,
          s5_log_step, w_glu, w_branch_sb, w_branch_s5, w_out, norm_ffn, w_router, b_router,
          w_up, b_up, w_down, b_down, norm_final, out):
    ctx = ExitStack()
    with ctx:
        def sb(name, shape, dt=F32):
            return ctx.enter_context(nc.sbuf_tensor(name, shape, dt))

        def sem(name):
            return ctx.enter_context(nc.semaphore(name))

        ring = sb("ring", [P, RING, RW])
        xres = sb("xres", [P, NT, D])
        hT = sb("hT", [P, KC, T])
        qk_region = sb("qk_region", [P, 2048])
        v_region = sb("v_region", [P, 1024])
        uT = sb("uT", [P, 4, T])
        gate_region = sb("gate_region", [P, 4096])
        y_region = sb("y_region", [P, 3072])
        s5_region = sb("s5_region", [P, 6144])
        BT = sb("BT", [P, 2, 4, P])
        c_region = sb("c_region", [P, 1536])
        CT = c_region[:, :].rearrange("p (w c n) -> p w c n", w=3, c=4)
        gain = sb("gain", [P, D])
        att_region = sb("att_region", [P, 2304])
        ident = sb("ident", [P, P])
        neg_tri = sb("neg_tri", [P, P])
        neg_ones = sb("neg_ones", [P, P])
        tri_bf = sb("tri_bf", [P, P], BF16)
        ones_bf = sb("ones_bf", [P, P], BF16)
        parT = sb("parT", [P, 5, PAIRS])
        pidx = sb("pidx", [P, 3], I32)
        gmask = sb("gmask", [P, 4])
        dcol = sb("dcol", [P, 4])
        stat = sb("stat", [P, 8])
        rowsel = sb("rowsel", [P, SLOTS])

        def win(slot):
            return ring[:, 2 * slot:2 * slot + 2, :].rearrange("p a (k n) -> p (a k) n", n=512)

        glu_w = ring[:, 0, :].rearrange("p (k n) -> p k n", n=512)
        sb_w = ring[:, 2:4, :].rearrange("p a (k n) -> p (a k) n", n=D)
        s5_w = ring[:, 4:6, :].rearrange("p a (k n) -> p (a k) n", n=D)
        out_w = ring[:, 8:12, :].rearrange("p a (k n) -> p (a k) n", n=D)
        cosT = ring[:, 8:10, :].rearrange("p a (j t) -> p (a j) t", t=T)
        sinT = ring[:, 10:12, :].rearrange("p a (j t) -> p (a j) t", t=T)

        qkT = qk_region[:, :].rearrange("p (c t) -> p c t", t=T)
        vtok = v_region[:, :].rearrange("p (a n) -> p a n", a=NT)
        bup = qk_region[0:E, :]
        bdn = v_region[0:E, :]
        xn = gate_region[:, 0:2048].rearrange("p (a n) -> p a n", a=NT)
        gT = gate_region[:, :].rearrange("p (c t) -> p c t", t=T)
        h2 = xn
        tab_dve = gate_region[:, 2048:4096].rearrange("p (a j t) -> p a j t", a=2, t=P)
        tab_pool = att_region[:, 0:2048].rearrange("p (a j t) -> p a j t", a=2, t=P)
        ysbT = y_region[:, 0:1024].rearrange("p (c t) -> p c t", t=T)
        ygT = y_region[:, 1024:2048].rearrange("p (c t) -> p c t", t=T)
        ys5T = y_region[:, 2048:3072].rearrange("p (c t) -> p c t", t=T)
        par = y_region[0:PAIRS, :].rearrange("p (i n) -> p i n", n=P)
        s5b = s5_region[:, :].rearrange("p (i b n) -> p i b n", i=6, b=2)
        b_raw = s5_region[:, 0:512].rearrange("p (r j h) -> p r j h", r=2, h=GCH)
        b_bar = s5_region[:, 512:1024].rearrange("p (r j h) -> p r j h", r=2, h=GCH)
        b_tmp = s5_region[:, 1024:1536].rearrange("p (r j h) -> p r j h", r=2, h=GCH)
        b_pad = s5_region[:, 1536:2560].rearrange("p (r j g h) -> p r j g h", r=2, g=2, h=GCH)
        c_raw = s5_region[:, 2560:3072].rearrange("p (r c n) -> p r c n", r=2, n=NSTATE)
        c_pad = s5_region[:, 3072:4096].rearrange("p (r c g n) -> p r c g n", r=2, g=2, n=NSTATE)
        gel = att_region[:, 0:1024].rearrange("p (i t) -> p i t", t=T)
        mrg = s5_region[:, 0:2048].rearrange("p (b n) -> p b n", n=512)
        att = att_region[:, :].rearrange("p (i b n) -> p i b n", i=3, b=2)
        sgl = s5_region[:, 2048:3072].rearrange("p (b n) -> p b n", n=512)

        hbf = s5_region[:, 0:3072].bitcast(BF16).rearrange("p (i a n) -> p i a n", i=3, a=NT)
        xT = s5_region[:, 3072:3584]
        actT = s5_region[:, 3584:4096]
        yslot = s5_region[:, 4096:4608]
        gsel = s5_region[:, 4608:4864].rearrange("p (a t) -> p a t", a=NT)
        pgate = s5_region[:, 4864:5120].rearrange("p (a s) -> p a s", a=NT)
        ponehot = s5_region[:, 5120:5184].bitcast(BF16).rearrange("p (a s) -> p a s", a=NT)
        glu, sig = gate_region[:, 2048:2560], gate_region[:, 2560:3072]
        lin, actv = gate_region[:, 3072:3584], gate_region[:, 3584:4096]
        rank_x = c_region[:, 0:NT * NV].rearrange("p (a v) -> p a v", a=NT)
        gate_x = c_region[:, 512:512 + NT * NV].rearrange("p (a v) -> p a v", a=NT)
        rt = c_region[:, 1024:1024 + 6 * NT * E].rearrange("p (i a e) -> p i a e", i=6, a=NT)
        iota_e = sb("iota_e", [P, E])
        iota_s = sb("iota_s", [P, 2 * SLOTS])
        wr = sb("wr", [P, KC, E])
        br = sb("br", [P, E])
        rtop = sb("rtop", [P, NT, 8])
        ridx = sb("ridx", [P, NT, 8], U32)
        ridxf = sb("ridxf", [P, NT, 8])
        mask_bf = sb("mask_bf", [P, NT, E], BF16)
        rsmall = sb("rsmall", [P, 8])
        rounds_i = sb("rounds_i", [P, 1], I32)
        gateT = uT[0:E, 0, :]

        bank = [ctx.enter_context(nc.psum_tensor(f"bank{i}", [P, 512], F32)) for i in range(8)]

        x_in = sem("x_in")
        gain_in = sem("gain_in")
        par_in = sem("par_in")
        bc_in = sem("bc_in")
        win_in = [sem(f"win_in{i}") for i in range(WIN_SLOTS)]
        mixw_in = [sem(f"mixw_in{i}") for i in range(4)]
        bias_in = sem("bias_in")
        rw_in = sem("rw_in")
        chunk_in = [sem(f"chunk_in{i}") for i in range(RING)]
        consts = sem("consts")
        idx_ready = sem("idx_ready")
        pool_step = sem("pool_step")
        dve_step = sem("dve_step")
        act_step = sem("act_step")
        sq_done = sem("sq_done")
        inv_done = sem("inv_done")
        rstd_done = sem("rstd_done")
        xn_done = sem("xn_done")
        step_done = sem("step_done")
        arg_done = sem("arg_done")
        absa_done = sem("absa_done")
        trig_done = sem("trig_done")
        par_done = sem("par_done")
        parT_psum = sem("parT_psum")
        parT_done = sem("parT_done")
        seed_done = sem("seed_done")
        table_pool = sem("table_pool")
        table_dve = sem("table_dve")
        bpad_done = sem("bpad_done")
        bT_psum = sem("bT_psum")
        bT_done = sem("bT_done")
        hT_psum = sem("hT_psum")
        hT_act = sem("hT_act")
        hT_dve = sem("hT_dve")
        proj_done = sem("proj_done")
        proj_read = sem("proj_read")
        bu_done = sem("bu_done")
        bu_read = sem("bu_read")
        mrot_done = sem("mrot_done")
        scan_done = sem("scan_done")
        pcos_done = sem("pcos_done")
        psin_done = sem("psin_done")
        ys5_psum = sem("ys5_psum")
        ys5_read = sem("ys5_read")
        gelu_arg = sem("gelu_arg")
        gelu_sig = sem("gelu_sig")
        yg_done = sem("yg_done")
        z_psum = sem("z_psum")
        absz_done = sem("absz_done")
        ln_done = sem("ln_done")
        sp_raw = sem("sp_raw")
        sp_done = sem("sp_done")
        expo_psum = sem("expo_psum")
        w_raw = sem("w_raw")
        w_done = sem("w_done")
        ysb_psum = sem("ysb_psum")
        ysb_done = sem("ysb_done")
        gates_done = sem("gates_done")
        glu_psum = sem("glu_psum")
        glu_sig = sem("glu_sig")
        ys5_done = sem("ys5_done")
        br_psum = sem("br_psum")
        br_read = sem("br_read")
        merged = sem("merged")
        mix_psum = sem("mix_psum")
        x1_done = sem("x1_done")
        h2_done = sem("h2_done")
        h2T_psum = sem("h2T_psum")
        h2T_act = sem("h2T_act")
        h2T_dve = sem("h2T_dve")
        hi_done = sem("hi_done")
        split_done = sem("split_done")
        logit_psum = sem("logit_psum")
        logit_sh = sem("logit_sh")
        exp_done = sem("exp_done")
        mask_done = sem("mask_done")
        rank_psum = sem("rank_psum")
        gates_ready = sem("gates_ready")
        gateT_psum = sem("gateT_psum")
        gateT_done = sem("gateT_done")
        rounds_ready = sem("rounds_ready")
        onehot_ready = sem("onehot_ready")
        gathered = sem("gathered")
        xT_ready = sem("xT_ready")
        bias_row = sem("bias_row")
        chunk_used = sem("chunk_used")
        up_done = sem("up_done")
        glu_ready = sem("glu_ready")
        lin_ready = sem("lin_ready")
        sig_ready = sem("sig_ready")
        prod_ready = sem("prod_ready")
        act_ready = sem("act_ready")
        actT_psum = sem("actT_psum")
        actT_ready = sem("actT_ready")
        pgate_ready = sem("pgate_ready")
        gsel_psum = sem("gsel_psum")
        gsel_ready = sem("gsel_ready")
        y_ready = sem("y_ready")
        scattered = sem("scattered")
        out_done = sem("out_done")
        stored = sem("stored")

        up_chunks = w_up.rearrange("l e (k p) n -> (l e k) p n", p=P)
        dn_chunks = w_down.rearrange("l e (k c p) n -> (l e k) p c n", p=P, c=2)

        MB = [0, 1, 6, 7]

        block = ctx.enter_context(nc.Block())

        @block.sync
        def _(sp):
            sp.dma_start(xres[:, :, :], x[0].rearrange("(a p) n -> p a n", p=P)).then_inc(x_in, 16)
            win_src = w_in[0].rearrange("(k p) n -> p k n", p=P)
            for i, g in enumerate(GROUP_ORDER):
                if i >= WIN_SLOTS:
                    sp.wait_ge(proj_done, 2 * (i - WIN_SLOTS + 1))
                sp.dma_start(win(i % WIN_SLOTS), win_src[:, :, g * 512:(g + 1) * 512])\
                  .then_inc(win_in[i % WIN_SLOTS], 16)
                if i == 1:
                    sp.wait_ge(xn_done, NT)
                    sp.dma_start(gain[:, :], norm_ffn.partition_broadcast(P)).then_inc(gain_in, 16)
                    sp.dma_start(wr[:, :, :], w_router[0].rearrange("(k p) n -> p k n", p=P))\
                      .then_inc(rw_in, 16)
                    sp.dma_start(br[:, :], b_router.partition_broadcast(P)).then_inc(rw_in, 16)
            sp.wait_ge(proj_done, 10)
            sp.dma_start(glu_w, w_glu[0].rearrange("(k p) n -> p k n", p=P)).then_inc(mixw_in[0], 16)
            sp.dma_start(ring[:, 1, :], up_chunks[1]).then_inc(chunk_in[1], 16)
            sp.wait_ge(proj_done, 12)
            sp.dma_start(sb_w, w_branch_sb[0].rearrange("(k p) n -> p k n", p=P)).then_inc(mixw_in[1], 16)
            sp.wait_ge(proj_done, 14)
            sp.dma_start(s5_w, w_branch_s5[0].rearrange("(k p) n -> p k n", p=P)).then_inc(mixw_in[2], 16)
            sp.wait_ge(proj_done, 16)
            for c in (6, 7):
                sp.dma_start(ring[:, c, :], up_chunks[c]).then_inc(chunk_in[c], 16)
            sp.wait_ge(pcos_done, PAIRS)
            sp.wait_ge(psin_done, PAIRS)
            sp.dma_start(out_w, w_out[0].rearrange("(k p) n -> p k n", p=P)).then_inc(mixw_in[3], 16)
            sp.wait_ge(glu_psum, 2)
            sp.dma_start(ring[:, 0, :], up_chunks[0]).then_inc(chunk_in[0], 16)
            sp.wait_ge(ysb_psum, HEADS)
            sp.dma_start(bup, b_up[0]).then_inc(bias_in, 16)
            sp.dma_start(bdn, b_down[0]).then_inc(bias_in, 16)
            sp.wait_ge(br_psum, 8)
            for c in (2, 3, 4, 5):
                sp.dma_start(ring[:, c, :], up_chunks[c]).then_inc(chunk_in[c], 16)
            sp.wait_ge(mix_psum, 4)
            for c in range(DNC):
                sp.dma_start(ring[:, UPC + c, :].rearrange("p (c n) -> p c n", c=2), dn_chunks[c])\
                  .then_inc(chunk_in[UPC + c], 16)

            def load_expert(v, e):
                for c in range(RING):
                    sp.wait_ge(chunk_used, v * RING - RING + c + 1)
                    if c < UPC:
                        sp.dma_start(ring[:, c, :], up_chunks[e * UPC + c]).then_inc(chunk_in[c], 16)
                    else:
                        sp.dma_start(ring[:, c, :].rearrange("p (c n) -> p c n", c=2),
                                     dn_chunks[e * DNC + c - UPC]).then_inc(chunk_in[c], 16)

            with sp.Fori(1, E) as e:
                load_expert(e, e)
            sp.wait_ge(h2_done, NT)
            sp.dma_start(gain[:, :], norm_final.partition_broadcast(P)).then_inc(gain_in, 16)
            sp.wait_ge(rounds_ready, 1)
            rounds = sp.value_load(rounds_i[0:1, 0:1], min_val=1, max_val=MAXR)
            with sp.If(rounds > 1):
                with sp.Fori(1, rounds) as r:
                    with sp.Fori(0, E) as e:
                        load_expert(r * E + e, e)
            out_v = out[0].rearrange("(a p) n -> p a n", p=P)
            for a in range(NT):
                sp.wait_ge(out_done, a + 1)
                sp.dma_start(out_v[:, a, :], xres[:, a, :]).then_inc(stored, 16)
            sp.wait_ge(stored, 16 * NT)

        def build_table(eng, link, js, tmp):
            k = js.stop - js.start
            filled = 1
            while filled < T:
                c, s = cosT[:, js, 0:filled], sinT[:, js, 0:filled]
                c2, s2 = cosT[:, js, filled:2 * filled], sinT[:, js, filled:2 * filled]
                cn = cosT[:, js, filled - 1:filled].to_broadcast([P, k, filled])
                sn = sinT[:, js, filled - 1:filled].to_broadcast([P, k, filled])
                a, b = tmp[:, 0, 0:k, 0:filled], tmp[:, 1, 0:k, 0:filled]
                link(eng.tensor_tensor(a, c, cn, ALU.mult))
                link(eng.tensor_tensor(b, s, sn, ALU.mult))
                link(eng.tensor_tensor(c2, a, b, ALU.subtract))
                link(eng.tensor_tensor(a, s, cn, ALU.mult))
                link(eng.tensor_tensor(b, c, sn, ALU.mult))
                link(eng.tensor_tensor(s2, a, b, ALU.add))
                filled *= 2

        @block.gpsimd
        def _(pool):
            n = [0]

            def link(ins):
                n[0] += 1
                ins.then_inc(pool_step, 1)
                pool.wait_ge(pool_step, n[0])

            def clear_where(t, pattern, op, base, cm, fill):
                return nc.gpsimd.affine_select(out=t, in_=t, compare_op=op, fill=fill, base=base,
                                               pattern=pattern, channel_multiplier=cm)

            link(nc.gpsimd.memset(ident[:, :], 0.0))
            clear_where(ident[:, :], [[-1, P]], ALU.not_equal, 0, 1, 1.0).then_inc(consts, 1)
            nc.gpsimd.iota(pidx[:, 0:1], pattern=[[0, 1]], base=0, channel_multiplier=1).then_inc(idx_ready, 1)
            link(nc.gpsimd.memset(neg_tri[:, :], -1.0))
            clear_where(neg_tri[:, :], [[-1, P]], ALU.is_ge, 0, 1, 0.0).then_inc(consts, 1)
            nc.gpsimd.memset(neg_ones[:, :], -1.0).then_inc(consts, 1)
            link(nc.gpsimd.memset(tri_bf[:, :], 1.0))
            clear_where(tri_bf[:, :], [[1, P]], ALU.is_gt, 0, -1, 0.0).then_inc(consts, 1)
            nc.gpsimd.memset(ones_bf[:, :], 1.0).then_inc(consts, 1)
            nc.gpsimd.iota(iota_e[:, :], pattern=[[1, E]], base=0, channel_multiplier=0,
                           allow_small_or_imprecise_dtypes=True).then_inc(consts, 1)
            nc.gpsimd.iota(iota_s[:, :], pattern=[[0, 2], [1, SLOTS]], base=0, channel_multiplier=0,
                           allow_small_or_imprecise_dtypes=True).then_inc(consts, 1)

            pool.wait_ge(seed_done, 2)
            build_table(nc.gpsimd, link, slice(PAIRS // 2, PAIRS), tab_pool)
            nc.gpsimd.memset(stat[:, 7:8], 0.0).then_inc(table_pool, 1)

            def rotate_in(j):
                b = j % 2
                t1, t2, m = s5b[:, 0, b, :], s5b[:, 1, b, :], s5b[:, 2, b, :]
                pool.wait_ge(bu_read, 2 * (j + 1))
                if j >= 2:
                    pool.wait_ge(scan_done, 2 * (j - 1))
                nc.gpsimd.tensor_tensor(m[:, 0:T], t1[:, 0:T], t2[:, T:2 * T], ALU.add).then_inc(mrot_done, 1)
                nc.gpsimd.tensor_tensor(m[:, T:2 * T], t1[:, T:2 * T], t2[:, 0:T], ALU.subtract)\
                  .then_inc(mrot_done, 1)

            def rotate_out(j):
                b = j % 2
                sc, p2 = s5b[:, 3, b, :], s5b[:, 5, b, :]
                pool.wait_ge(scan_done, 2 * (j + 1))
                if j >= 2:
                    pool.wait_ge(ys5_psum, j - 1)
                nc.gpsimd.tensor_tensor(p2.rearrange("p (r t) -> p r t", r=2),
                                        sc.rearrange("p (r t) -> p r t", r=2),
                                        sinT[:, j:j + 1, :].to_broadcast([P, 2, T]), ALU.mult)\
                  .then_inc(psin_done, 1)

            def mask_sp(h):
                pool.wait_ge(sp_raw, h + 1)
                spt = att[:, 1, h % 2, :].rearrange("p (i t) -> p i t", t=P)[:, 0:3:2, :]
                clear_where(spt, [[0, 2], [1, P]], ALU.is_gt, 0, -1, 0.0).then_inc(sp_done, 1)

            def mask_w(h):
                pool.wait_ge(w_raw, h + 1)
                wt = att[:, 2, h % 2, :].rearrange("p (i t) -> p i t", t=P)[:, 0:3:2, :]
                clear_where(wt, [[0, 2], [1, P]], ALU.is_gt, 0, -1, 0.0).then_inc(w_done, 1)

            done = 0
            for n_half in range(NHALF):
                upto = s5_steps_after(n_half)
                for s in range(done, upto):
                    if s < PAIRS:
                        rotate_in(s)
                    if 1 <= s <= PAIRS:
                        rotate_out(s - 1)
                done = upto
                if n_half >= ATT_FROM:
                    h = n_half - ATT_FROM
                    mask_sp(h)
                    if h >= 1:
                        mask_w(h - 1)
            mask_w(HEADS - 1)

            def pick_row(v, e):
                pool.wait_ge(up_done, v)
                nc.gpsimd.tensor_copy(rowsel[0:E, :], ident[0:E, bass.ds(e, 1)].to_broadcast([E, SLOTS]))\
                  .then_inc(bias_row, 1)

            nc.gpsimd.tensor_copy(rowsel[0:E, :], ident[0:E, 0:1].to_broadcast([E, SLOTS])).then_inc(bias_row, 1)
            with pool.Fori(1, E) as e:
                pick_row(e, e)
            pool.wait_ge(rounds_ready, 1)
            rounds = pool.value_load(rounds_i[0:1, 0:1], min_val=1, max_val=MAXR)
            with pool.If(rounds > 1):
                with pool.Fori(1, rounds) as r:
                    with pool.Fori(0, E) as e:
                        pick_row(r * E + e, e)

        @block.scalar
        def _(act):
            act.dma_start(par[:, 0, :], s5_lam_re[0].rearrange("(j g) p -> j (g p)", g=2)).then_inc(par_in, 16)
            act.dma_start(par[:, 1, :], s5_lam_im[0].rearrange("(j g) p -> j (g p)", g=2)).then_inc(par_in, 16)
            act.dma_start(par[:, 2, 0:2], s5_log_step[0].rearrange("(j g) -> j g", g=2)).then_inc(par_in, 16)
            act.dma_start(gain[:, :], norm_mix.partition_broadcast(P)).then_inc(gain_in, 16)
            for r, (b_src, c_src) in enumerate(((s5_b_re, s5_c_re), (s5_b_im, s5_c_im))):
                act.dma_start(b_raw[:, r], b_src[0].rearrange("(j g) p h -> (g p) j h", g=2)).then_inc(bc_in, 16)
                act.dma_start(c_raw[:, r], c_src[0].rearrange("(c g) h n -> (g h) c n", g=8)).then_inc(bc_in, 16)
            act.dma_start(par[0:4, 15, :], s5_d[0].rearrange("(c g) h -> c (g h)", g=8)).then_inc(par_in, 16)

            act.wait_ge(par_in, 64)
            nc.scalar.activation(par[:, 3, 0:2], par[:, 2, 0:2], ACT.Exp).then_inc(step_done, 1)
            act.wait_ge(x_in, 16)
            for a in range(NT):
                nc.scalar.activation(xn[:, a, :], xres[:, a, :], ACT.Square, accum_out=stat[:, a:a + 1])\
                  .then_inc(sq_done, 1)
            act.wait_ge(inv_done, 1)
            nc.scalar.activation(stat[:, 4:6], stat[:, 2:4], ACT.Sqrt).then_inc(rstd_done, 1)
            act.wait_ge(arg_done, 1)
            nc.scalar.activation(par[:, 6, :], par[:, 4, :], ACT.Exp).then_inc(trig_done, 1)
            act.wait_ge(absa_done, 1)
            nc.scalar.activation(par[:, 8, :], par[:, 5, :], ACT.Sin).then_inc(trig_done, 1)
            nc.scalar.activation(par[:, 7, :], par[:, 9, :], ACT.Sin).then_inc(trig_done, 1)

            for b in range(2):
                act.wait_ge(hT_psum, b + 1)
                nc.scalar.activation(hT[:, 2 * b:2 * b + 2, :].rearrange("p c t -> p (c t)"),
                                     bank[b][:, :], ACT.Copy).then_inc(hT_act, 1)

            def drain_proj(n):
                g, half = GROUP_ORDER[n // 2], n % 2
                act.wait_ge(proj_done, n + 1)
                src = bank[n % 2][:, :]
                if g == 3:
                    dst, scale = uT[:, 2 * half:2 * half + 2, :].rearrange("p c t -> p (c t)"), 1.0
                elif g == 2:
                    dst, scale = vtok[:, half, :], 1.0
                elif g < 2:
                    c = 4 * g + 2 * half
                    dst, scale = qkT[:, c:c + 2, :].rearrange("p c t -> p (c t)"), (HD ** -0.5 if g == 0 else 1.0)
                else:
                    c = 4 * (g - 4) + 2 * half
                    if n == 8:
                        act.wait_ge(table_dve, 1)
                    dst, scale = gT[:, c:c + 2, :].rearrange("p c t -> p (c t)"), 1.0
                nc.scalar.activation(dst, src, ACT.Copy, scale=scale).then_inc(proj_read, 1)

            def soften(h):
                a = att[:, 0, h % 2, :]
                act.wait_ge(z_psum, h + 1)
                if h == 0:
                    act.wait_ge(table_pool, 1)
                if h >= 2:
                    act.wait_ge(sp_raw, h - 1)
                nc.scalar.activation(a, bank[2 + h % 2][:, 0:384], ACT.Abs).then_inc(absz_done, 1)
                act.wait_ge(absz_done, 3 * h + 1)
                nc.scalar.activation(a, a, ACT.Exp, scale=-1.0).then_inc(absz_done, 1)
                act.wait_ge(absz_done, 3 * h + 2)
                nc.scalar.activation(a, a, ACT.Ln, bias=1.0).then_inc(absz_done, 1)

            def weights(h):
                act.wait_ge(expo_psum, h + 1)
                if h >= 2:
                    act.wait_ge(ysb_psum, h - 1)
                nc.scalar.activation(att[:, 2, h % 2, :], bank[2 + h % 2][:, 0:384], ACT.Exp).then_inc(w_raw, 1)

            def drain_ysb(i):
                act.wait_ge(ysb_psum, 2 * i + 2)
                nc.scalar.activation(ysbT[:, i, :], bank[7][:, 0:T], ACT.Copy).then_inc(ysb_done, 1)

            act.wait_ge(parT_psum, 1)
            for n in range(NHALF):
                drain_proj(n)
                if n >= ATT_FROM:
                    h = n - ATT_FROM
                    if h >= 4 and h % 2 == 0:
                        drain_ysb(h // 2 - 2)
                    soften(h)
                    if h >= 1:
                        weights(h - 1)
            drain_ysb(HEADS // 2 - 2)
            weights(HEADS - 1)
            drain_ysb(HEADS // 2 - 1)
            act.wait_ge(proj_read, NHALF)
            nc.scalar.activation(gate_region[:, :], gate_region[:, :], ACT.Sigmoid).then_inc(gates_done, 1)
            for c in range(4):
                act.wait_ge(gelu_arg, c + 1)
                nc.scalar.activation(gel[:, 3, :], gel[:, 2, :], ACT.Sigmoid, scale=GELU_S).then_inc(gelu_sig, 1)
            for i in range(2):
                act.wait_ge(glu_psum, i + 1)
                nc.scalar.activation(sgl[:, i, :], bank[i][:, :], ACT.Sigmoid).then_inc(glu_sig, 1)

            for a in range(NT):
                act.wait_ge(x1_done, 2 * (a + 1))
                nc.scalar.activation(h2[:, a, :], xres[:, a, :], ACT.Square, accum_out=stat[:, a:a + 1])\
                  .then_inc(sq_done, 1)
            act.wait_ge(inv_done, 2)
            nc.scalar.activation(stat[:, 4:6], stat[:, 2:4], ACT.Sqrt).then_inc(rstd_done, 1)
            for a in range(NT):
                act.wait_ge(h2_done, a + 1)
                nc.scalar.activation(hbf[:, 0, a, :], h2[:, a, :], ACT.Copy).then_inc(hi_done, 1)
            for b in range(2):
                act.wait_ge(h2T_psum, b + 1)
                nc.scalar.activation(hT[:, 2 * b:2 * b + 2, :].rearrange("p c t -> p (c t)"),
                                     bank[b][:, :], ACT.Copy).then_inc(h2T_act, 1)
            act.wait_ge(logit_sh, 1)
            nc.scalar.activation(rt[:, 2, :, :], rt[:, 5, :, :], ACT.Exp).then_inc(exp_done, 1)
            act.wait_ge(gateT_psum, 1)
            nc.scalar.activation(gateT, bank[6][0:E, 0:T], ACT.Copy).then_inc(gateT_done, 1)

            def drain_gather(v):
                act.wait_ge(gathered, v + 1)
                nc.scalar.activation(xT, bank[6][:, :], ACT.Copy).then_inc(xT_ready, 1)

            def expert(v):
                act.wait_ge(glu_ready, v + 1)
                nc.scalar.activation(sig, glu, ACT.Sigmoid, scale=ALPHA).then_inc(sig_ready, 1)
                drain_gather(v + 1)
                act.wait_ge(gsel_psum, v + 1)
                nc.scalar.activation(gsel.rearrange("p a t -> p (a t)"), bank[7][:, 0:T], ACT.Copy)\
                  .then_inc(gsel_ready, 1)

            drain_gather(0)
            with act.Fori(0, E) as v:
                expert(v)
            act.wait_ge(rounds_ready, 1)
            rounds = act.value_load(rounds_i[0:1, 0:1], min_val=1, max_val=MAXR)
            with act.If(rounds > 1):
                with act.Fori(1, rounds) as r:
                    with act.Fori(0, E) as e:
                        expert(r * E + e)

            for a in range(NT):
                act.wait_ge(x1_done, 4 + 2 * (a + 1))
                nc.scalar.activation(h2[:, a, :], xres[:, a, :], ACT.Square, accum_out=stat[:, a:a + 1])\
                  .then_inc(sq_done, 1)
            act.wait_ge(inv_done, 3)
            nc.scalar.activation(stat[:, 4:6], stat[:, 2:4], ACT.Sqrt).then_inc(rstd_done, 1)

        @block.vector
        def _(dve):
            n = [0]

            def link(ins):
                n[0] += 1
                ins.then_inc(dve_step, 1)
                dve.wait_ge(dve_step, n[0])

            V = nc.vector

            def inverse_mean_square(k):
                dve.wait_ge(sq_done, NT * k)
                link(V.tensor_scalar(stat[:, 0:2], stat[:, 0:2], 1.0 / D, EPS, ALU.mult, ALU.add))
                V.reciprocal(stat[:, 2:4], stat[:, 0:2]).then_inc(inv_done, 1)

            def norm(k, dst, done):
                dve.wait_ge(rstd_done, k)
                dve.wait_ge(gain_in, 16 * k)
                for a in range(NT):
                    V.scalar_tensor_tensor(dst[:, a, :], xres[:, a, :], stat[:, 4 + a:5 + a], gain[:, :],
                                           ALU.mult, ALU.mult).then_inc(done, 1)

            step = par[:, 3, 0:2].unsqueeze(2).to_broadcast([PAIRS, 2, NSTATE])

            def pv(i):
                return par[:, i, :].rearrange("p (g n) -> p g n", g=2)

            dve.wait_ge(step_done, 1)
            V.tensor_tensor(pv(4), pv(0), step, ALU.mult).then_inc(arg_done, 1)
            link(V.tensor_tensor(pv(5), pv(1), step, ALU.mult))
            link(V.tensor_scalar(par[:, 10, :], par[:, 5, :], 1.0 / TWO_PI, None, ALU.mult))
            link(V.tensor_scalar(par[:, 10, :], par[:, 10, :], MAGIC, None, ALU.add))
            link(V.tensor_scalar(par[:, 10, :], par[:, 10, :], MAGIC, None, ALU.subtract))
            for part in (PI_A, PI_B, PI_C):
                link(V.scalar_tensor_tensor(par[:, 5, :], par[:, 10, :], -part, par[:, 5, :],
                                            ALU.mult, ALU.add))
            link(V.tensor_scalar(par[:, 5, :], par[:, 5, :], 3.1415925, -3.1415925, ALU.min, ALU.max))
            link(V.scalar_tensor_tensor(par[:, 9, :], par[:, 5, :], -1.0, par[:, 5, :], ALU.mult, ALU.max))
            V.tensor_scalar(par[:, 9, :], par[:, 9, :], -1.0, TWO_PI / 4, ALU.mult, ALU.add)\
             .then_inc(absa_done, 1)

            inverse_mean_square(1)
            norm(1, xn, xn_done)

            for b in (2, 3):
                dve.wait_ge(hT_psum, b + 1)
                V.tensor_copy(hT[:, 2 * b:2 * b + 2, :].rearrange("p c t -> p (c t)"), bank[b][:, :])\
                 .then_inc(hT_dve, 1)

            dve.wait_ge(trig_done, 3)
            link(V.tensor_tensor(par[:, 10, :], par[:, 6, :], par[:, 7, :], ALU.mult))
            link(V.tensor_scalar(par[:, 10, :], par[:, 10, :], 1.0, None, ALU.subtract))
            link(V.tensor_tensor(par[:, 11, :], par[:, 6, :], par[:, 8, :], ALU.mult))
            link(V.tensor_tensor(par[:, 12, :], par[:, 0, :], par[:, 0, :], ALU.mult))
            link(V.tensor_tensor(par[:, 13, :], par[:, 1, :], par[:, 1, :], ALU.mult))
            link(V.tensor_tensor(par[:, 12, :], par[:, 12, :], par[:, 13, :], ALU.add))
            link(V.reciprocal(par[:, 12, :], par[:, 12, :]))
            link(V.tensor_tensor(par[:, 13, :], par[:, 10, :], par[:, 0, :], ALU.mult))
            link(V.tensor_tensor(par[:, 14, :], par[:, 11, :], par[:, 1, :], ALU.mult))
            link(V.tensor_tensor(par[:, 13, :], par[:, 13, :], par[:, 14, :], ALU.add))
            link(V.tensor_tensor(par[:, 9, :], par[:, 13, :], par[:, 12, :], ALU.mult))
            link(V.tensor_tensor(par[:, 13, :], par[:, 11, :], par[:, 0, :], ALU.mult))
            link(V.tensor_tensor(par[:, 14, :], par[:, 10, :], par[:, 1, :], ALU.mult))
            link(V.tensor_tensor(par[:, 13, :], par[:, 13, :], par[:, 14, :], ALU.subtract))
            V.tensor_tensor(par[:, 10, :], par[:, 13, :], par[:, 12, :], ALU.mult).then_inc(par_done, 1)
            dve.wait_ge(par_done, 1)
            dve.wait_ge(parT_psum, 1)
            V.tensor_copy(parT[:, :, :].rearrange("p i j -> p (i j)"), bank[6][:, 0:5 * PAIRS])\
             .then_inc(parT_done, 1)
            V.tensor_copy(dcol[:, :], bank[6][:, 5 * PAIRS:5 * PAIRS + 4]).then_inc(parT_done, 1)
            dve.wait_ge(parT_done, 2)
            V.tensor_copy(cosT[:, :, 0:1], parT[:, 1, :].unsqueeze(2)).then_inc(seed_done, 1)
            V.tensor_copy(sinT[:, :, 0:1], parT[:, 2, :].unsqueeze(2)).then_inc(seed_done, 1)

            dve.wait_ge(idx_ready, 1)
            link(V.tensor_scalar(pidx[:, 1:2], pidx[:, 0:1], 6, 1, ALU.arith_shift_right, ALU.bitwise_and))
            link(V.tensor_scalar(pidx[:, 2:3], pidx[:, 0:1], 4, 1, ALU.arith_shift_right, ALU.bitwise_and))
            link(V.tensor_copy(gmask[:, 1:4:2], pidx[:, 1:3]))
            link(V.tensor_scalar(gmask[:, 0:3:2], gmask[:, 1:4:2], -1.0, 1.0, ALU.mult, ALU.add))

            dve.wait_ge(bc_in, 64)
            f = [parT[:, 3 + r, :].unsqueeze(2).to_broadcast([P, PAIRS, GCH]) for r in range(2)]
            link(V.tensor_tensor(b_bar[:, 0], b_raw[:, 0], f[0], ALU.mult))
            link(V.tensor_tensor(b_tmp[:, 0], b_raw[:, 1], f[1], ALU.mult))
            link(V.tensor_tensor(b_bar[:, 0], b_bar[:, 0], b_tmp[:, 0], ALU.subtract))
            link(V.tensor_tensor(b_bar[:, 1], b_raw[:, 1], f[0], ALU.mult))
            link(V.tensor_tensor(b_tmp[:, 1], b_raw[:, 0], f[1], ALU.mult))
            link(V.tensor_tensor(b_bar[:, 1], b_bar[:, 1], b_tmp[:, 1], ALU.add))
            for r in range(2):
                for g in range(2):
                    V.tensor_scalar(b_pad[:, r, :, g, :], b_bar[:, r], gmask[:, g:g + 1], None, ALU.mult)\
                     .then_inc(bpad_done, 1)
            for r in range(2):
                for g in range(2):
                    V.tensor_scalar(c_pad[:, r, :, g, :], c_raw[:, r], gmask[:, 2 + g:3 + g], None, ALU.mult)\
                     .then_inc(bpad_done, 1)
            for r in range(2):
                dve.wait_ge(bT_psum, r + 1)
                V.tensor_copy(BT[:, r].rearrange("p c n -> p (c n)"), bank[4 + r][:, :]).then_inc(bT_done, 1)
            dve.wait_ge(bT_psum, 3)
            V.tensor_copy(CT[:, 0].rearrange("p c n -> p (c n)"), bank[7][:, :]).then_inc(bT_done, 1)
            V.tensor_scalar(CT[:, 1].rearrange("p c n -> p (c n)"), bank[7][:, :], -1.0, None, ALU.mult)\
             .then_inc(bT_done, 1)
            dve.wait_ge(bT_psum, 4)
            V.tensor_scalar(CT[:, 2].rearrange("p c n -> p (c n)"), bank[6][:, :], -1.0, None, ALU.mult)\
             .then_inc(bT_done, 1)

            dve.wait_ge(seed_done, 2)
            dve.wait_ge(xn_done, NT)
            build_table(V, link, slice(0, PAIRS // 2), tab_dve)
            V.memset(stat[:, 6:7], 0.0).then_inc(table_dve, 1)

            def two(ap):
                return ap.rearrange("p (r t) -> p r t", r=2)

            def rotate_in(j):
                b = j % 2
                if j == PAIRS // 2:
                    dve.wait_ge(table_pool, 1)
                dve.wait_ge(bu_done, 2 * (j + 1))
                if j >= 2:
                    dve.wait_ge(mrot_done, 2 * (j - 1))
                for i, table in enumerate((cosT, sinT)):
                    V.tensor_tensor(two(s5b[:, i, b, :]), two(bank[4 + b][:, :]),
                                    table[:, j:j + 1, :].to_broadcast([P, 2, T]), ALU.mult)\
                     .then_inc(bu_read, 1)

            def scan(j):
                b = j % 2
                m, sc = s5b[:, 2, b, :], s5b[:, 3, b, :]
                mag = parT[:, 0, j:j + 1].to_broadcast([P, T])
                dve.wait_ge(mrot_done, 2 * (j + 1))
                if j >= 2:
                    dve.wait_ge(psin_done, j - 1)
                    dve.wait_ge(ys5_psum, j - 1)
                for r in range(2):
                    V.tensor_tensor_scan(sc[:, r * T:(r + 1) * T], mag, m[:, r * T:(r + 1) * T], 0.0,
                                         ALU.mult, ALU.add).then_inc(scan_done, 1)
                dve.wait_ge(scan_done, 2 * (j + 1))
                V.tensor_tensor(two(s5b[:, 4, b, :]), two(sc),
                                cosT[:, j:j + 1, :].to_broadcast([P, 2, T]), ALU.mult).then_inc(pcos_done, 1)

            def softplus(h):
                dve.wait_ge(absz_done, 3 * (h + 1))
                if h >= 2:
                    dve.wait_ge(expo_psum, h - 1)
                V.scalar_tensor_tensor(att[:, 1, h % 2, :], bank[2 + h % 2][:, 0:384], 0.0,
                                       att[:, 0, h % 2, :], ALU.max, ALU.add).then_inc(sp_raw, 1)

            def drain_s5(c):
                dve.wait_ge(ys5_psum, CW * (c + 1))
                V.scalar_tensor_tensor(ygT[:, c, :], uT[:, c, :], dcol[:, c:c + 1],
                                       bank[6][:, 0:T], ALU.mult, ALU.add)\
                 .then_inc(ys5_read, 1)

            done = 0
            for n_half in range(NHALF):
                upto = s5_steps_after(n_half)
                for s in range(done, upto):
                    if s >= 6 and (s - 6) % CW == 0:
                        drain_s5((s - 6) // CW)
                    if s < PAIRS:
                        rotate_in(s)
                    if 1 <= s <= PAIRS:
                        scan(s - 1)
                done = upto
                if n_half >= ATT_FROM:
                    softplus(n_half - ATT_FROM)

            drain_s5(3)
            dve.wait_ge(w_done, HEADS)
            dve.wait_ge(ysb_psum, HEADS)
            dve.wait_ge(ys5_read, 4)
            for c in range(4):
                y = ygT[:, c, :]
                link(V.tensor_tensor(gel[:, 1, :], y, y, ALU.mult))
                link(V.tensor_scalar(gel[:, 1, :], gel[:, 1, :], GELU_C, 1.0, ALU.mult, ALU.add))
                V.tensor_tensor(gel[:, 2, :], gel[:, 1, :], y, ALU.mult).then_inc(gelu_arg, 1)
                dve.wait_ge(gelu_sig, c + 1)
                V.tensor_tensor(y, y, gel[:, 3, :], ALU.mult).then_inc(yg_done, 1)

            for i in range(2):
                dve.wait_ge(glu_sig, i + 1)
                V.tensor_tensor(ys5T[:, 2 * i:2 * i + 2, :].rearrange("p c t -> p (c t)"),
                                ygT[:, 2 * i:2 * i + 2, :].rearrange("p c t -> p (c t)"),
                                sgl[:, i, :], ALU.mult).then_inc(ys5_done, 1)

            dve.wait_ge(gates_done, 1)
            for m in range(KC):
                dve.wait_ge(br_psum, m + 1)
                link(V.tensor_tensor(two(mrg[:, m % 2, :]), two(bank[2 + m % 4][:, :]), gT[:, m:m + 9:8, :],
                                     ALU.mult))
                V.tensor_tensor(hT[:, m, :], mrg[:, m % 2, 0:T], mrg[:, m % 2, T:2 * T], ALU.add)\
                 .then_inc(merged, 1)

            for i in range(4):
                a, c = i // 2, i % 2
                dve.wait_ge(mix_psum, i + 1)
                V.tensor_tensor(xres[:, a, c * 512:(c + 1) * 512], xres[:, a, c * 512:(c + 1) * 512],
                                bank[MB[i]][:, :], ALU.add).then_inc(x1_done, 1)
            inverse_mean_square(2)
            norm(2, h2, h2_done)

            for b in (2, 3):
                dve.wait_ge(h2T_psum, b + 1)
                V.tensor_copy(hT[:, 2 * b:2 * b + 2, :].rearrange("p c t -> p (c t)"), bank[b][:, :])\
                 .then_inc(h2T_dve, 1)

            lg, mk, ex, gt, rk, scr = (rt[:, i] for i in range(6))
            dve.wait_ge(rw_in, 32)
            dve.wait_ge(consts, 7)
            dve.wait_ge(logit_psum, 1)
            link(V.tensor_tensor(lg, bank[4][:, 0:NT * E].rearrange("p (a e) -> p a e", a=NT),
                                 br[:, :].unsqueeze(1).to_broadcast([P, NT, E]), ALU.add))
            for a in range(NT):
                link(V.max(rtop[:, a, :], lg[:, a, :]))
            link(V.tensor_tensor(scr, lg, rtop[:, :, 0:1].to_broadcast([P, NT, E]), ALU.subtract))
            V.memset(rsmall[:, 0:1], 0.0).then_inc(logit_sh, 1)
            for a in range(NT):
                link(V.max_index(ridx[:, a, :], rtop[:, a, :], lg[:, a, :]))
            link(V.tensor_copy(ridxf[:, :, :], ridx[:, :, :]))
            for k in range(TOPK):
                for a in range(NT):
                    if k == 0:
                        last = V.tensor_scalar(mk[:, a, :], iota_e[:, :], ridxf[:, a, 0:1], None, ALU.is_equal)
                    else:
                        last = V.scalar_tensor_tensor(mk[:, a, :], iota_e[:, :], ridxf[:, a, k:k + 1],
                                                      mk[:, a, :], ALU.is_equal, ALU.add)
                    link(last)
            V.tensor_copy(mask_bf[:, :, :], mk).then_inc(mask_done, 1)
            dve.wait_ge(exp_done, 1)
            link(V.tensor_tensor(ex, ex, mk, ALU.mult))
            link(V.tensor_reduce(rsmall[:, 1:3], ex, AX.X, ALU.add))
            link(V.reciprocal(rsmall[:, 3:5], rsmall[:, 1:3]))
            V.tensor_tensor(gt, ex, rsmall[:, 3:5].unsqueeze(2).to_broadcast([P, NT, E]), ALU.mult)\
             .then_inc(gates_ready, 1)
            dve.wait_ge(gates_ready, 1)
            dve.wait_ge(rank_psum, 1)
            link(V.tensor_scalar(rk, mk, -NOT_ROUTED, NOT_ROUTED, ALU.mult, ALU.add))
            link(V.tensor_tensor(rk, rk, bank[5][:, 0:NT * E].rearrange("p (a e) -> p a e", a=NT), ALU.add))
            link(V.reduce_max(rsmall[:, 5:6], bank[5][:, NT * E:NT * E + E], AX.X))
            for r in range(MAXR + 1):
                w = min(E, NV - r * E)
                link(V.tensor_scalar(rank_x[:, :, r * E:r * E + w], rk[:, :, 0:w], float(r * SLOTS), None,
                                     ALU.subtract))
                link(V.tensor_copy(gate_x[:, :, r * E:r * E + w], gt[:, :, 0:w]))

            def one_hot(v):
                dve.wait_ge(gathered, v)
                for a in range(NT):
                    V.tensor_scalar(ponehot[:, a, :], iota_s[:, 0:SLOTS], rank_x[:, a, bass.ds(v, 1)], None,
                                    ALU.is_equal).then_inc(onehot_ready, 1)

            for a in range(NT):
                V.tensor_scalar(ponehot[:, a, :], iota_s[:, 0:SLOTS], rank_x[:, a, 0:1], None,
                                ALU.is_equal).then_inc(onehot_ready, 1)

            for a in range(NT):
                dve.wait_ge(hi_done, a + 1)
                link(V.tensor_tensor(h2[:, a, :], h2[:, a, :], hbf[:, 0, a, :], ALU.subtract))
                link(V.tensor_copy(hbf[:, 1, a, :], h2[:, a, :]))
                V.tensor_tensor(hbf[:, 2, a, :], h2[:, a, :], hbf[:, 1, a, :], ALU.subtract)\
                 .then_inc(split_done, 1)

            link(V.tensor_scalar(rsmall[:, 6:7], rsmall[:, 5:6], float(SLOTS), 1.0, ALU.is_gt, ALU.add))
            for r in range(2, MAXR):
                link(V.scalar_tensor_tensor(rsmall[:, 6:7], rsmall[:, 5:6], float(r * SLOTS), rsmall[:, 6:7],
                                            ALU.is_gt, ALU.add))
            V.tensor_copy(rounds_i[:, :], rsmall[:, 6:7]).then_inc(rounds_ready, 1)
            V.memset(yslot, 0.0).then_inc(y_ready, 1)
            V.memset(gsel, 0.0).then_inc(y_ready, 1)

            def expert(v):
                for a in range(NT):
                    V.tensor_scalar(pgate[:, a, :], iota_s[:, :], rank_x[:, a, bass.ds(v, 1)],
                                    gate_x[:, a, bass.ds(v, 1)], ALU.is_equal, ALU.mult)\
                     .then_inc(pgate_ready, 1)
                one_hot(v + 1)
                dve.wait_ge(up_done, v + 1)
                V.tensor_scalar(glu, bank[4][:, :], LIMIT, None, ALU.min).then_inc(glu_ready, 1)
                V.tensor_scalar(lin, bank[5][:, :], LIMIT, -LIMIT, ALU.min, ALU.max).then_inc(lin_ready, 1)
                dve.wait_ge(sig_ready, v + 1)
                dve.wait_ge(glu_ready, v + 1)
                V.tensor_tensor(glu, glu, sig, ALU.mult).then_inc(prod_ready, 1)
                dve.wait_ge(lin_ready, v + 1)
                dve.wait_ge(prod_ready, v + 1)
                V.scalar_tensor_tensor(actv, lin, 1.0, glu, ALU.add, ALU.mult).then_inc(act_ready, 1)
                dve.wait_ge(actT_psum, v + 1)
                V.tensor_copy(actT, bank[6][:, :]).then_inc(actT_ready, 1)
                dve.wait_ge(chunk_used, v * RING + RING)
                V.tensor_copy(yslot, bank[7][:, :]).then_inc(y_ready, 1)

            with dve.Fori(0, E) as v:
                expert(v)
            dve.wait_ge(rounds_ready, 1)
            rounds = dve.value_load(rounds_i[0:1, 0:1], min_val=1, max_val=MAXR)
            with dve.If(rounds > 1):
                with dve.Fori(1, rounds) as r:
                    with dve.Fori(0, E) as e:
                        expert(r * E + e)

            dve.wait_ge(mix_psum, 5)
            for i in range(4):
                a, c = i // 2, i % 2
                V.tensor_tensor(xres[:, a, c * 512:(c + 1) * 512], xres[:, a, c * 512:(c + 1) * 512],
                                bank[i][:, :], ALU.add).then_inc(x1_done, 1)
            inverse_mean_square(3)
            norm(3, xres, out_done)

        @block.tensor
        def _(pe):
            M = nc.tensor

            pe.wait_ge(consts, 1)
            for b in range(4):
                for kc in (2 * b, 2 * b + 1):
                    for a in range(NT):
                        pe.wait_ge(xn_done, a + 1)
                        last = M.transpose(bank[b][:, (kc % 2) * T + a * P:(kc % 2) * T + (a + 1) * P],
                                           xn[:, a, kc * P:(kc + 1) * P], ident[:, :])
                last.then_inc(hT_psum, 1)
            pe.wait_ge(par_done, 1)
            for i in range(5):
                last = M.transpose(bank[6][:, i * PAIRS:(i + 1) * PAIRS], par[:, 6 + i, :],
                                   ident[0:PAIRS, 0:PAIRS])
            last = M.transpose(bank[6][:, 5 * PAIRS:5 * PAIRS + 4], par[0:4, 15, :], ident[0:4, 0:4])
            last.then_inc(parT_psum, 1)

            def project(n):
                i, half = n // 2, n % 2
                g, w = GROUP_ORDER[i], win(i % WIN_SLOTS)
                if half == 0:
                    pe.wait_ge(win_in[i % WIN_SLOTS], 16 * (i // WIN_SLOTS + 1))
                if n >= 2:
                    pe.wait_ge(proj_read, n - 1)
                o = bank[n % 2]
                if g == 2:
                    for kc in range(KC):
                        last = M.matmul(o[:, :], hT[:, kc, half * P:(half + 1) * P], w[:, kc, :],
                                        start=(kc == 0), stop=(kc == KC - 1))
                else:
                    for c in range(2):
                        m = 2 * half + c
                        for kc in range(KC):
                            last = M.matmul(o[:, c * T:(c + 1) * T], w[:, kc, m * P:(m + 1) * P], hT[:, kc, :],
                                            start=(kc == 0), stop=(kc == KC - 1))
                last.then_inc(proj_done, 1)

            def bu(j):
                c, r0 = j // CW, 32 * (j % CW)
                if j >= 2:
                    pe.wait_ge(bu_read, 2 * (j - 1))
                for r in range(2):
                    M.matmul(bank[4 + j % 2][:, r * T:(r + 1) * T], BT[r0:r0 + 32, r, c, :],
                             uT[r0:r0 + 32, c, :], start=True, stop=True).then_inc(bu_done, 1)

            def s5_out(j):
                c, r0, b = j // CW, 32 * (j % CW), j % 2
                pe.wait_ge(pcos_done, j + 1)
                pe.wait_ge(psin_done, j + 1)
                if c >= 1 and j % CW == 0:
                    pe.wait_ge(ys5_read, c)
                o = bank[6][r0:r0 + 32, 0:T]
                pc, ps = s5b[:, 4, b, :], s5b[:, 5, b, :]
                terms = ((0, pc[:, 0:T]), (1, ps[:, T:2 * T]), (2, ps[:, 0:T]), (2, pc[:, T:2 * T]))
                for i, (w, rhs) in enumerate(terms):
                    last = M.matmul(o, CT[:, w, c, r0:r0 + 32], rhs, start=(i == 0), stop=(i == 3))
                last.then_inc(ys5_psum, 1)

            def scores(h):
                r0, c = HD * (h % 2), h // 2
                q, k = qkT[r0:r0 + HD, c, :], qkT[r0:r0 + HD, 4 + c, :]
                if h >= 2:
                    pe.wait_ge(w_raw, h - 1)
                z = bank[2 + h % 2]
                M.matmul(z[:, 0:T], k[:, 0:P], q, start=True, stop=True)
                M.matmul(z[:, T:T + P], k[:, P:T], q[:, P:T], start=False, stop=True, skip_group_check=True)\
                 .then_inc(z_psum, 1)

            def exponents(h):
                pe.wait_ge(sp_done, h + 1)
                z, spt = bank[2 + h % 2], att[:, 1, h % 2, :]
                M.matmul(z[:, 0:T], neg_tri[:, :], spt[:, 0:T], start=False, stop=True,
                         skip_group_check=True)
                M.matmul(z[:, P:T], neg_ones[:, :], spt[:, T:T + P], start=False, stop=True,
                         skip_group_check=True)
                M.matmul(z[:, T:T + P], neg_tri[:, :], spt[:, T:T + P], start=False, stop=True,
                         skip_group_check=True)\
                 .then_inc(expo_psum, 1)

            def attend(h):
                r0, i = HD * (h % 2), h // 2
                pe.wait_ge(w_done, h + 1)
                if h >= 2 and h % 2 == 0:
                    pe.wait_ge(ysb_done, i)
                w = att[:, 2, h % 2, :]
                o = bank[7][r0:r0 + HD, 0:T]
                M.matmul(o, vtok[:, 0, h * HD:(h + 1) * HD], w[:, 0:T], start=True, stop=False)
                M.matmul(o[:, P:T], vtok[:, 1, h * HD:(h + 1) * HD], w[:, T:T + P], start=False, stop=True)\
                 .then_inc(ysb_psum, 1)

            pe.wait_ge(hT_act, 2)
            pe.wait_ge(hT_dve, 2)
            project(0)
            for r in range(2):
                pe.wait_ge(bpad_done, 2 * (r + 1))
                for c in range(4):
                    last = M.transpose(bank[4 + r][:, c * P:(c + 1) * P],
                                       b_pad[:, r, CW * c:CW * (c + 1)].rearrange("p j g h -> p (j g h)"),
                                       ident[:, :])
                last.then_inc(bT_psum, 1)
            pe.wait_ge(parT_done, 2)
            for r in range(2):
                pe.wait_ge(bpad_done, 4 + 2 * (r + 1))
                for c in range(4):
                    last = M.transpose(bank[7 - r][:, c * P:(c + 1) * P],
                                       c_pad[:, r, c].rearrange("p g n -> p (g n)"), ident[:, :])
                last.then_inc(bT_psum, 1)
            for n in range(1, NHALF):
                project(n)
                if n == S5_FROM:
                    pe.wait_ge(bT_done, 5)
                    pe.wait_ge(proj_read, 2)
                for s in range(s5_steps_after(n - 1), s5_steps_after(n)):
                    if s < PAIRS:
                        bu(s)
                    if s >= 2:
                        s5_out(s - 2)
                if n == ATT_FROM:
                    pe.wait_ge(consts, 3)
                    pe.wait_ge(proj_read, 8)
                if n >= ATT_FROM:
                    h = n - ATT_FROM
                    scores(h)
                    if h >= 1:
                        exponents(h - 1)
                    if h >= 2:
                        attend(h - 2)
            exponents(HEADS - 1)
            attend(HEADS - 2)
            attend(HEADS - 1)

            pe.wait_ge(mixw_in[0], 16)
            pe.wait_ge(yg_done, 4)
            pe.wait_ge(proj_read, NHALF)
            for i in range(2):
                for c in range(2):
                    m = 2 * i + c
                    for kc in range(4):
                        last = M.matmul(bank[i][:, c * T:(c + 1) * T], glu_w[:, kc, m * P:(m + 1) * P],
                                        ygT[:, kc, :], start=(kc == 0), stop=(kc == 3))
                last.then_inc(glu_psum, 1)

            pe.wait_ge(mixw_in[1], 16)
            pe.wait_ge(mixw_in[2], 16)
            pe.wait_ge(ysb_done, HEADS // 2)
            pe.wait_ge(ys5_done, 2)
            for m in range(KC):
                if m >= 4:
                    pe.wait_ge(merged, m - 3)
                for c, (w, y) in enumerate(((sb_w, ysbT), (s5_w, ys5T))):
                    for kc in range(4):
                        last = M.matmul(bank[2 + m % 4][:, c * T:(c + 1) * T], w[:, kc, m * P:(m + 1) * P],
                                        y[:, kc, :], start=(kc == 0), stop=(kc == 3))
                last.then_inc(br_psum, 1)

            pe.wait_ge(mixw_in[3], 16)
            pe.wait_ge(ys5_read, 4)
            for i in range(4):
                a, c = i // 2, i % 2
                for kc in range(KC):
                    pe.wait_ge(merged, kc + 1)
                    last = M.matmul(bank[MB[i]][:, :], hT[:, kc, a * P:(a + 1) * P],
                                    out_w[:, kc, c * 512:(c + 1) * 512], start=(kc == 0), stop=(kc == KC - 1))
                last.then_inc(mix_psum, 1)

            for b in range(4):
                for kc in (2 * b, 2 * b + 1):
                    for a in range(NT):
                        pe.wait_ge(h2_done, a + 1)
                        last = M.transpose(bank[b][:, (kc % 2) * T + a * P:(kc % 2) * T + (a + 1) * P],
                                           h2[:, a, kc * P:(kc + 1) * P], ident[:, :])
                last.then_inc(h2T_psum, 1)
            pe.wait_ge(h2T_act, 2)
            pe.wait_ge(h2T_dve, 2)
            pe.wait_ge(rw_in, 32)
            for a in range(NT):
                for kc in range(KC):
                    last = M.matmul(bank[4][:, a * E:(a + 1) * E], hT[:, kc, a * P:(a + 1) * P], wr[:, kc, :],
                                    start=(kc == 0), stop=(kc == KC - 1))
            last.then_inc(logit_psum, 1)
            pe.wait_ge(mask_done, 1)
            pe.wait_ge(consts, 5)
            M.matmul(bank[5][:, 0:E], tri_bf[:, :], mask_bf[:, 0, :], start=True, stop=True)
            M.matmul(bank[5][:, E:2 * E], ones_bf[:, :], mask_bf[:, 0, :], start=True, stop=False)
            M.matmul(bank[5][:, E:2 * E], tri_bf[:, :], mask_bf[:, 1, :], start=False, stop=True)
            M.matmul(bank[5][:, 2 * E:3 * E], ones_bf[:, :], mask_bf[:, 0, :], start=True, stop=False)
            M.matmul(bank[5][:, 2 * E:3 * E], ones_bf[:, :], mask_bf[:, 1, :], start=False, stop=True)\
             .then_inc(rank_psum, 1)
            pe.wait_ge(gates_ready, 1)
            for a in range(NT):
                last = M.transpose(bank[6][0:E, a * P:(a + 1) * P], rt[:, 3, a, :], ident[:, :])
            last.then_inc(gateT_psum, 1)
            pe.wait_ge(gateT_done, 1)
            pe.wait_ge(bias_in, 32)
            for a in range(NT):
                for c in range(2):
                    M.matmul(bank[2 * a + c][:, :], gateT[:, a * P:(a + 1) * P], bdn[:, c * 512:(c + 1) * 512],
                             start=True, stop=False)

            def gather(v):
                pe.wait_ge(onehot_ready, (v + 1) * NT)
                for kc in range(KC):
                    k = 0
                    for i in range(3):
                        for a in range(NT):
                            last = M.matmul(bank[6][:, kc * SLOTS:(kc + 1) * SLOTS],
                                            hbf[:, i, a, kc * P:(kc + 1) * P], ponehot[:, a, :],
                                            start=(k == 0), stop=(k == 3 * NT - 1))
                            k += 1
                last.then_inc(gathered, 1)

            def scatter(v, stop=False):
                pe.wait_ge(y_ready, v + 2)
                for a in range(NT):
                    for c in range(2):
                        r = slice(SLOTS * c, SLOTS * (c + 1))
                        last = M.matmul(bank[2 * a + c][:, :], gsel[r, a, :], yslot[r, :],
                                        start=False, stop=stop)
                return last

            def expert(v):
                pe.wait_ge(xT_ready, v + 1)
                for k in range(UPC):
                    pe.wait_ge(chunk_in[k], (v + 1) * 16)
                    for q in range(4):
                        r = SLOTS * (q % 2)
                        last = M.matmul(bank[4 + q // 2][r:r + SLOTS, :], xT[:, k * SLOTS:(k + 1) * SLOTS],
                                        ring[:, k, q * 512:(q + 1) * 512], start=(k == 0), stop=False)
                    last.then_inc(chunk_used, 1)
                pe.wait_ge(bias_row, v + 1)
                for q in range(4):
                    r = SLOTS * (q % 2)
                    last = M.matmul(bank[4 + q // 2][r:r + SLOTS, :], rowsel[0:E, :],
                                    bup[:, q * 512:(q + 1) * 512], start=False, stop=True)
                last.then_inc(up_done, 1)
                scatter(v).then_inc(scattered, 1)
                gather(v + 1)
                pe.wait_ge(pgate_ready, (v + 1) * NT)
                for a in range(NT):
                    last = M.transpose(bank[7][:, a * P:(a + 1) * P], pgate[:, a, :], ident[:, :])
                last.then_inc(gsel_psum, 1)
                pe.wait_ge(act_ready, v + 1)
                pe.wait_ge(xT_ready, v + 2)
                for j in range(4):
                    last = M.transpose(bank[6][:, j * P:(j + 1) * P], actv[:, j * P:(j + 1) * P], ident[:, :])
                last.then_inc(actT_psum, 1)
                pe.wait_ge(actT_ready, v + 1)
                pe.wait_ge(gsel_ready, v + 1)
                for k in range(KC):
                    if k % 2 == 0:
                        pe.wait_ge(chunk_in[UPC + k // 2], (v + 1) * 16)
                    f = (k % 4) * P + (k // 4) * SLOTS
                    for c in range(2):
                        r, n0 = SLOTS * c, (k % 2) * D + c * 512
                        last = M.matmul(bank[7][r:r + SLOTS, :], actT[:, f:f + SLOTS],
                                        ring[:, UPC + k // 2, n0:n0 + 512], start=(k == 0), stop=(k == KC - 1))
                    if k % 2 == 1:
                        last.then_inc(chunk_used, 1)

            pe.wait_ge(split_done, NT)
            gather(0)
            with pe.Fori(0, E) as v:
                expert(v)
            pe.wait_ge(rounds_ready, 1)
            rounds = pe.value_load(rounds_i[0:1, 0:1], min_val=1, max_val=MAXR)
            with pe.If(rounds > 1):
                with pe.Fori(1, rounds) as r:
                    with pe.Fori(0, E) as e:
                        expert(r * E + e)
            scatter(rounds * E, stop=True).then_inc(mix_psum, 1)


_INS = ['x', 'norm_mix', 'w_in', 's5_lam_re', 's5_lam_im', 's5_b_re', 's5_b_im', 's5_c_re', 's5_c_im',
        's5_d', 's5_log_step', 'w_glu', 'w_branch_sb', 'w_branch_s5', 'w_out', 'norm_ffn', 'w_router',
        'b_router', 'w_up', 'b_up', 'w_down', 'b_down', 'norm_final']


def kernel(**inputs):
    import numpy as np
    import concourse.bacc as bacc
    from concourse.bass_utils import run_bass_kernel_spmd

    nc = bacc.Bacc("TRN2", target_bir_lowering=False, num_devices=1)
    arrays, args = {}, []
    for name in _INS:
        a = np.ascontiguousarray(inputs[name])
        arrays[f"in_{name}"] = a
        args.append(nc.dram_tensor(f"in_{name}", a.shape, mybir.dt.from_np(a.dtype), kind="ExternalInput").ap())
    out = nc.dram_tensor("out", (1, T, D), F32, kind="ExternalOutput").ap()
    build(nc, *args, out)
    r = run_bass_kernel_spmd(nc, [arrays], core_ids=[0])
    return r.results[0]["out"]
```

```python
from contextlib import ExitStack

import concourse.bass as bass
from concourse import mybir

F32 = mybir.dt.float32
BF16 = mybir.dt.bfloat16
I32 = mybir.dt.int32
U32 = mybir.dt.uint32
ALU = mybir.AluOpType
ACT = mybir.ActivationFunctionType
AX = mybir.AxisListType

P = 128
T = 256
NT = T // P
D = 1024
KC = D // P
HEADS, HD = 8, 64
GROUPS, GCH, NSTATE = 32, 16, 64
PAIRS = GROUPS // 2
CW = 4
E = 32
TOPK = 4
FF = 1024
SLOTS = 64
MAXR = T // SLOTS
NV = MAXR * E + 1
UPC = KC
DNC = KC // 2
RING = UPC + DNC
RW = 2 * FF
EPS = 1e-5
LIMIT, ALPHA = 7.0, 1.702
TWO_PI = 6.283185307179586
PI_A = 6.28125
PI_B = 0.0019353071693331003
PI_C = 1.02520991e-11
MAGIC = 12582912.0
GELU_C = 0.044715
GELU_S = 1.5957691216057308
NOT_ROUTED = 4096.0

GROUP_ORDER = [3, 0, 1, 2, 4, 5, 6, 7]
NHALF = 2 * len(GROUP_ORDER)
WIN_SLOTS = 4
UNITS = 2 * NHALF
BT_AFTER = 5
S5_FROM, S5_STEPS = 10, PAIRS + 2
ATT_FROM, ATT_STEPS = 13, HEADS + 2


def s5_step(u):
    return u - S5_FROM if 0 <= u - S5_FROM < S5_STEPS else None


def att_step(u):
    t, odd = divmod(u - ATT_FROM, 2)
    return t if not odd and 0 <= t < ATT_STEPS else None


def build(nc, x, norm_mix, w_in, s5_lam_re, s5_lam_im, s5_b_re, s5_b_im, s5_c_re, s5_c_im, s5_d,
          s5_log_step, w_glu, w_branch_sb, w_branch_s5, w_out, norm_ffn, w_router, b_router,
          w_up, b_up, w_down, b_down, norm_final, out):
    ctx = ExitStack()
    with ctx:
        def sb(name, shape, dt=F32):
            return ctx.enter_context(nc.sbuf_tensor(name, shape, dt))

        def sem(name):
            return ctx.enter_context(nc.semaphore(name))

        ring = sb("ring", [P, RING, RW])
        xres = sb("xres", [P, NT, D])
        hT = sb("hT", [P, KC, T])
        qk_region = sb("qk_region", [P, 2048])
        v_region = sb("v_region", [P, 1024])
        uT = sb("uT", [P, 4, T])
        gate_region = sb("gate_region", [P, 4096])
        y_region = sb("y_region", [P, 3072])
        s5_region = sb("s5_region", [P, 6144])
        BT = sb("BT", [P, 2, 4, P])
        c_region = sb("c_region", [P, 1536])
        CT = c_region[:, 0:1024].rearrange("p (w c n) -> p w c n", w=2, c=4)
        gain = sb("gain", [P, D])
        att_region = sb("att_region", [P, 2304])
        ident = sb("ident", [P, P])
        neg_tri = sb("neg_tri", [P, P])
        neg_ones = sb("neg_ones", [P, P])
        tri_bf = sb("tri_bf", [P, P], BF16)
        ones_bf = sb("ones_bf", [P, P], BF16)
        parT = sb("parT", [P, 5, PAIRS])
        pidx = sb("pidx", [P, 3], I32)
        gmask = sb("gmask", [P, 4])
        dcol = sb("dcol", [P, 4])
        stat = sb("stat", [P, 12])
        rowsel = sb("rowsel", [P, SLOTS])

        def win(slot):
            return ring[:, 2 * slot:2 * slot + 2, :].rearrange("p a (k n) -> p (a k) n", n=512)

        glu_w = ring[:, 0, :].rearrange("p (k n) -> p k n", n=512)
        sb_w = ring[:, 2:4, :].rearrange("p a (k n) -> p (a k) n", n=D)
        s5_w = ring[:, 4:6, :].rearrange("p a (k n) -> p (a k) n", n=D)
        out_w = ring[:, 8:12, :].rearrange("p a (k n) -> p (a k) n", n=D)
        cosT = ring[:, 8:10, :].rearrange("p a (j t) -> p (a j) t", t=T)
        sinT = ring[:, 10:12, :].rearrange("p a (j t) -> p (a j) t", t=T)

        qkT = qk_region[:, :].rearrange("p (c t) -> p c t", t=T)
        vtok = v_region[:, :].rearrange("p (a n) -> p a n", a=NT)
        bup = qk_region[0:E, :]
        bdn = v_region[0:E, :]
        xn = gate_region[:, 0:2048].rearrange("p (a n) -> p a n", a=NT)
        gT = gate_region[:, :].rearrange("p (c t) -> p c t", t=T)
        h2 = xn
        tab_dve = gate_region[:, 2048:4096].rearrange("p (a j t) -> p a j t", a=2, t=P)
        tab_pool = att_region[:, 0:2048].rearrange("p (a j t) -> p a j t", a=2, t=P)
        ysbT = y_region[:, 0:1024].rearrange("p (c t) -> p c t", t=T)
        ygT = y_region[:, 1024:2048].rearrange("p (c t) -> p c t", t=T)
        ys5T = y_region[:, 2048:3072].rearrange("p (c t) -> p c t", t=T)
        par = y_region[0:PAIRS, :].rearrange("p (i n) -> p i n", n=P)
        s5b = s5_region[:, :].rearrange("p (i b n) -> p i b n", i=6, b=2)
        b_raw = s5_region[:, 0:512].rearrange("p (r j h) -> p r j h", r=2, h=GCH)
        b_bar = s5_region[:, 512:1024].rearrange("p (r j h) -> p r j h", r=2, h=GCH)
        b_tmp = s5_region[:, 1024:1536].rearrange("p (r j h) -> p r j h", r=2, h=GCH)
        b_pad = s5_region[:, 1536:2560].rearrange("p (r j g h) -> p r j g h", r=2, g=2, h=GCH)
        c_raw = s5_region[:, 2560:3072].rearrange("p (r c n) -> p r c n", r=2, n=NSTATE)
        c_pad = s5_region[:, 3072:4096].rearrange("p (r c g n) -> p r c g n", r=2, g=2, n=NSTATE)
        gel = y_region[:, 2048:3072].rearrange("p (i n) -> p i n", i=2)
        mrg = s5_region[:, 0:2048].rearrange("p (b n) -> p b n", n=512)
        att = att_region[:, :].rearrange("p (i b n) -> p i b n", i=3, b=2)
        sq_junk = att_region[:, 1792:2304]
        sgl = s5_region[:, 2048:3072].rearrange("p (b n) -> p b n", n=512)

        hbf = s5_region[:, 0:3072].bitcast(BF16).rearrange("p (i a n) -> p i a n", i=3, a=NT)
        xT = s5_region[:, 3072:3584]
        actT = s5_region[:, 3584:4096]
        yslot = s5_region[:, 4096:4608]
        gsel = s5_region[:, 4608:4864].rearrange("p (a t) -> p a t", a=NT)
        pgate = s5_region[:, 4864:5120].rearrange("p (a s) -> p a s", a=NT)
        ponehot = s5_region[:, 5120:5184].bitcast(BF16).rearrange("p (a s) -> p a s", a=NT)
        glu, sig = gate_region[:, 2048:2560], gate_region[:, 2560:3072]
        lin, actv = gate_region[:, 3072:3584], gate_region[:, 3584:4096]
        rank_x = c_region[:, 0:NT * NV].rearrange("p (a v) -> p a v", a=NT)
        gate_x = c_region[:, 512:512 + NT * NV].rearrange("p (a v) -> p a v", a=NT)
        rt = c_region[:, 1024:1024 + 6 * NT * E].rearrange("p (i a e) -> p i a e", i=6, a=NT)
        iota_e = sb("iota_e", [P, E])
        iota_s = sb("iota_s", [P, 2 * SLOTS])
        wr = sb("wr", [P, KC, E])
        br = sb("br", [P, E])
        rtop = sb("rtop", [P, NT, 8])
        ridx = sb("ridx", [P, NT, 8], U32)
        ridxf = sb("ridxf", [P, NT, 8])
        hits = att_region[:, 0:NT * TOPK * E].rearrange("p (a k e) -> p a k e", a=NT, k=TOPK)
        mask_bf = sb("mask_bf", [P, NT, E], BF16)
        rsmall = sb("rsmall", [P, 8])
        rounds_i = sb("rounds_i", [P, 1], I32)
        gateT = uT[0:E, 0, :]

        bank = [ctx.enter_context(nc.psum_tensor(f"bank{i}", [P, 512], F32)) for i in range(8)]

        x_in = [sem(f"x_in{a}") for a in range(NT)]
        win_half = sem("win_half")
        gain_in = sem("gain_in")
        par_in = sem("par_in")
        bc_in = sem("bc_in")
        win_in = [sem(f"win_in{i}") for i in range(WIN_SLOTS)]
        mixw_in = [sem(f"mixw_in{i}") for i in range(4)]
        bias_in = sem("bias_in")
        rw_in = sem("rw_in")
        chunk_in = [sem(f"chunk_in{i}") for i in range(RING)]
        consts = sem("consts")
        idx_ready = sem("idx_ready")
        pool_step = sem("pool_step")
        dve_step = sem("dve_step")
        sq_done = sem("sq_done")
        inv_done = sem("inv_done")
        rstd_done = sem("rstd_done")
        xn_done = sem("xn_done")
        step_done = sem("step_done")
        arg_done = sem("arg_done")
        absa_done = sem("absa_done")
        trig_done = sem("trig_done")
        par_done = sem("par_done")
        parT_psum = sem("parT_psum")
        parT_done = sem("parT_done")
        seed_done = sem("seed_done")
        table_pool = sem("table_pool")
        table_dve = sem("table_dve")
        bpad_done = sem("bpad_done")
        bT_psum = sem("bT_psum")
        bT_done = sem("bT_done")
        hT_psum = sem("hT_psum")
        hT_act = sem("hT_act")
        hT_dve = sem("hT_dve")
        proj_done = sem("proj_done")
        proj_read = sem("proj_read")
        bu_done = sem("bu_done")
        bu_read = sem("bu_read")
        mrot_done = sem("mrot_done")
        scan_done = sem("scan_done")
        pcos_done = sem("pcos_done")
        psin_done = sem("psin_done")
        state_done = sem("state_done")
        ys5_psum = sem("ys5_psum")
        ys5_read = sem("ys5_read")
        gelu_arg = sem("gelu_arg")
        gelu_sig = sem("gelu_sig")
        yg_done = sem("yg_done")
        z_psum = sem("z_psum")
        absz_done = sem("absz_done")
        sp_raw = sem("sp_raw")
        sp_done = sem("sp_done")
        expo_psum = sem("expo_psum")
        w_raw = sem("w_raw")
        w_done = sem("w_done")
        ysb_psum = sem("ysb_psum")
        ysb_done = sem("ysb_done")
        gates_done = sem("gates_done")
        glu_psum = sem("glu_psum")
        glu_sig = sem("glu_sig")
        ys5_done = sem("ys5_done")
        br_psum = sem("br_psum")
        merged_sb = sem("merged_sb")
        merged = sem("merged")
        mix_psum = sem("mix_psum")
        x1_done = sem("x1_done")
        h2_done = sem("h2_done")
        h2T_psum = sem("h2T_psum")
        h2T_act = sem("h2T_act")
        h2T_dve = sem("h2T_dve")
        hi_done = sem("hi_done")
        mid_done = sem("mid_done")
        split_done = sem("split_done")
        logit_psum = sem("logit_psum")
        logit_sh = sem("logit_sh")
        exp_done = sem("exp_done")
        mask_done = sem("mask_done")
        rank_psum = sem("rank_psum")
        gates_ready = sem("gates_ready")
        gateT_psum = sem("gateT_psum")
        gateT_done = sem("gateT_done")
        rounds_ready = sem("rounds_ready")
        onehot_ready = sem("onehot_ready")
        gathered = sem("gathered")
        xT_ready = sem("xT_ready")
        bias_row = sem("bias_row")
        chunk_used = sem("chunk_used")
        up_done = sem("up_done")
        glu_ready = sem("glu_ready")
        lin_ready = sem("lin_ready")
        sig_ready = sem("sig_ready")
        prod_ready = sem("prod_ready")
        act_ready = sem("act_ready")
        actT_psum = sem("actT_psum")
        actT_ready = sem("actT_ready")
        pgate_ready = sem("pgate_ready")
        gsel_psum = sem("gsel_psum")
        gsel_ready = sem("gsel_ready")
        y_ready = sem("y_ready")
        out_done = sem("out_done")
        stored = sem("stored")

        up_chunks = w_up.rearrange("l e (k p) n -> (l e k) p n", p=P)
        dn_chunks = w_down.rearrange("l e (k c p) n -> (l e k) p c n", p=P, c=2)

        MB = [0, 1, 6, 7]

        block = ctx.enter_context(nc.Block())

        @block.sync
        def _(sp):
            x_src = x[0].rearrange("(a p) n -> p a n", p=P)
            for a in range(NT):
                sp.dma_start(xres[:, a, :], x_src[:, a, :]).then_inc(x_in[a], 16)
            sp.dma_start(gain[:, :], norm_mix.partition_broadcast(P)).then_inc(gain_in, 16)
            win_src = w_in[0].rearrange("(k p) n -> p k n", p=P)

            def load_win(i):
                g = GROUP_ORDER[i]
                sp.dma_start(win(i % WIN_SLOTS), win_src[:, :, g * 512:(g + 1) * 512])\
                  .then_inc(win_in[i % WIN_SLOTS], 16)

            g0 = GROUP_ORDER[0] * 512
            sp.dma_start(win(0)[:, :, 0:256], win_src[:, :, g0:g0 + 256]).then_inc(win_in[0], 16)
            sp.dma_start(win(0)[:, :, 256:512], win_src[:, :, g0 + 256:g0 + 512]).then_inc(win_half, 16)
            for r, (b_src, c_src) in enumerate(((s5_b_re, s5_c_re), (s5_b_im, s5_c_im))):
                sp.dma_start(b_raw[:, r], b_src[0].rearrange("(j g) p h -> (g p) j h", g=2)).then_inc(bc_in, 16)
                sp.dma_start(c_raw[:, r], c_src[0].rearrange("(c g) h n -> (g h) c n", g=8)).then_inc(bc_in, 16)
            for i in range(1, WIN_SLOTS):
                load_win(i)
            sp.wait_ge(xn_done, NT)
            sp.dma_start(gain[:, :], norm_ffn.partition_broadcast(P)).then_inc(gain_in, 16)
            sp.dma_start(wr[:, :, :], w_router[0].rearrange("(k p) n -> p k n", p=P)).then_inc(rw_in, 16)
            sp.dma_start(br[:, :], b_router.partition_broadcast(P)).then_inc(rw_in, 16)
            for i in range(WIN_SLOTS, len(GROUP_ORDER)):
                sp.wait_ge(proj_done, 2 * (i - WIN_SLOTS + 1))
                load_win(i)
            sp.wait_ge(proj_done, 10)
            sp.dma_start(glu_w, w_glu[0].rearrange("(k p) n -> p k n", p=P)).then_inc(mixw_in[0], 16)
            sp.dma_start(ring[:, 1, :], up_chunks[1]).then_inc(chunk_in[1], 16)
            sp.wait_ge(proj_done, 12)
            sp.dma_start(sb_w, w_branch_sb[0].rearrange("(k p) n -> p k n", p=P)).then_inc(mixw_in[1], 16)
            sp.wait_ge(proj_done, 14)
            sp.dma_start(s5_w, w_branch_s5[0].rearrange("(k p) n -> p k n", p=P)).then_inc(mixw_in[2], 16)
            sp.wait_ge(proj_done, 16)
            for c in (6, 7):
                sp.dma_start(ring[:, c, :], up_chunks[c]).then_inc(chunk_in[c], 16)
            sp.wait_ge(pcos_done, PAIRS)
            sp.wait_ge(psin_done, PAIRS)
            sp.dma_start(out_w, w_out[0].rearrange("(k p) n -> p k n", p=P)).then_inc(mixw_in[3], 16)
            sp.wait_ge(glu_psum, 2)
            sp.dma_start(ring[:, 0, :], up_chunks[0]).then_inc(chunk_in[0], 16)
            sp.wait_ge(ysb_psum, HEADS)
            sp.dma_start(bup, b_up[0]).then_inc(bias_in, 16)
            sp.dma_start(bdn, b_down[0]).then_inc(bias_in, 16)
            sp.wait_ge(br_psum, 8)
            for c in (2, 3, 4, 5):
                sp.dma_start(ring[:, c, :], up_chunks[c]).then_inc(chunk_in[c], 16)
            sp.wait_ge(mix_psum, 4)
            for c in range(DNC):
                sp.dma_start(ring[:, UPC + c, :].rearrange("p (c n) -> p c n", c=2), dn_chunks[c])\
                  .then_inc(chunk_in[UPC + c], 16)

            def load_expert(v, e):
                for c in range(RING):
                    sp.wait_ge(chunk_used, v * RING - RING + c + 1)
                    if c < UPC:
                        sp.dma_start(ring[:, c, :], up_chunks[e * UPC + c]).then_inc(chunk_in[c], 16)
                    else:
                        sp.dma_start(ring[:, c, :].rearrange("p (c n) -> p c n", c=2),
                                     dn_chunks[e * DNC + c - UPC]).then_inc(chunk_in[c], 16)

            with sp.Fori(1, E) as e:
                load_expert(e, e)
            sp.wait_ge(h2_done, 2 * NT)
            sp.dma_start(gain[:, :], norm_final.partition_broadcast(P)).then_inc(gain_in, 16)
            sp.wait_ge(rounds_ready, 1)
            rounds = sp.value_load(rounds_i[0:1, 0:1], min_val=1, max_val=MAXR)
            with sp.If(rounds > 1):
                with sp.Fori(1, rounds) as r:
                    with sp.Fori(0, E) as e:
                        load_expert(r * E + e, e)
            out_v = out[0].rearrange("(a p) n -> p a n", p=P)
            for i in range(2 * NT):
                a, n = i // 2, slice(i % 2 * 512, i % 2 * 512 + 512)
                sp.wait_ge(out_done, i + 1)
                sp.dma_start(out_v[:, a, n], xres[:, a, n]).then_inc(stored, 16)
            sp.wait_ge(stored, 2 * NT * 16)

        def build_table(eng, link, js, tmp):
            k = js.stop - js.start
            filled = 1
            while filled < T:
                c, s = cosT[:, js, 0:filled], sinT[:, js, 0:filled]
                c2, s2 = cosT[:, js, filled:2 * filled], sinT[:, js, filled:2 * filled]
                cn = cosT[:, js, filled - 1:filled].to_broadcast([P, k, filled])
                sn = sinT[:, js, filled - 1:filled].to_broadcast([P, k, filled])
                a, b = tmp[:, 0, 0:k, 0:filled], tmp[:, 1, 0:k, 0:filled]
                link(eng.tensor_tensor(a, c, cn, ALU.mult))
                link(eng.tensor_tensor(b, s, sn, ALU.mult))
                link(eng.tensor_tensor(c2, a, b, ALU.subtract))
                link(eng.tensor_tensor(a, s, cn, ALU.mult))
                link(eng.tensor_tensor(b, c, sn, ALU.mult))
                link(eng.tensor_tensor(s2, a, b, ALU.add))
                filled *= 2

        @block.gpsimd
        def _(pool):
            n = [0]

            def link(ins):
                n[0] += 1
                ins.then_inc(pool_step, 1)
                pool.wait_ge(pool_step, n[0])

            def clear_where(t, pattern, op, base, cm, fill):
                return nc.gpsimd.affine_select(out=t, in_=t, compare_op=op, fill=fill, base=base,
                                               pattern=pattern, channel_multiplier=cm)

            link(nc.gpsimd.memset(ident[:, :], 0.0))
            clear_where(ident[:, :], [[-1, P]], ALU.not_equal, 0, 1, 1.0).then_inc(consts, 1)
            nc.gpsimd.iota(pidx[:, 0:1], pattern=[[0, 1]], base=0, channel_multiplier=1).then_inc(idx_ready, 1)
            link(nc.gpsimd.memset(neg_tri[:, :], -1.0))
            clear_where(neg_tri[:, :], [[-1, P]], ALU.is_ge, 0, 1, 0.0).then_inc(consts, 1)
            nc.gpsimd.memset(neg_ones[:, :], -1.0).then_inc(consts, 1)
            link(nc.gpsimd.memset(tri_bf[:, :], 1.0))
            clear_where(tri_bf[:, :], [[1, P]], ALU.is_gt, 0, -1, 0.0).then_inc(consts, 1)
            nc.gpsimd.memset(ones_bf[:, :], 1.0).then_inc(consts, 1)
            nc.gpsimd.iota(iota_e[:, :], pattern=[[1, E]], base=0, channel_multiplier=0,
                           allow_small_or_imprecise_dtypes=True).then_inc(consts, 1)
            nc.gpsimd.iota(iota_s[:, :], pattern=[[0, 2], [1, SLOTS]], base=0, channel_multiplier=0,
                           allow_small_or_imprecise_dtypes=True).then_inc(consts, 1)

            pool.wait_ge(seed_done, 2)
            build_table(nc.gpsimd, link, slice(PAIRS // 2, PAIRS), tab_pool)
            nc.gpsimd.memset(stat[:, 11:12], 0.0).then_inc(table_pool, 1)

            def rotate_in(j):
                b = j % 2
                t1, t2, m = s5b[:, 0, b, :], s5b[:, 1, b, :], s5b[:, 2, b, :]
                pool.wait_ge(bu_read, 2 * (j + 1))
                if j >= 2:
                    pool.wait_ge(scan_done, 2 * (j - 1))
                nc.gpsimd.tensor_tensor(m[:, 0:T], t1[:, 0:T], t2[:, T:2 * T], ALU.add).then_inc(mrot_done, 1)
                nc.gpsimd.tensor_tensor(m[:, T:2 * T], t1[:, T:2 * T], t2[:, 0:T], ALU.subtract)\
                  .then_inc(mrot_done, 1)

            def rotate_out(j):
                b = j % 2
                sc, p2 = s5b[:, 3, b, :], s5b[:, 5, b, :]
                pool.wait_ge(scan_done, 2 * (j + 1))
                if j >= 2:
                    pool.wait_ge(state_done, 2 * (j - 1))
                nc.gpsimd.tensor_tensor(p2.rearrange("p (r t) -> p r t", r=2),
                                        sc.rearrange("p (r t) -> p r t", r=2),
                                        sinT[:, j:j + 1, :].to_broadcast([P, 2, T]), ALU.mult)\
                  .then_inc(psin_done, 1)

            def mask_sp(h):
                pool.wait_ge(sp_raw, h + 1)
                spt = att[:, 1, h % 2, :].rearrange("p (i t) -> p i t", t=P)[:, 0:3:2, :]
                clear_where(spt, [[0, 2], [1, P]], ALU.is_gt, 0, -1, 0.0).then_inc(sp_done, 1)

            def mask_w(h):
                pool.wait_ge(w_raw, h + 1)
                wt = att[:, 2, h % 2, :].rearrange("p (i t) -> p i t", t=P)[:, 0:3:2, :]
                clear_where(wt, [[0, 2], [1, P]], ALU.is_gt, 0, -1, 0.0).then_inc(w_done, 1)

            for u in range(UNITS):
                s = s5_step(u)
                if s is not None:
                    if s < PAIRS:
                        rotate_in(s)
                    if 1 <= s <= PAIRS:
                        rotate_out(s - 1)
                t = att_step(u)
                if t is not None:
                    if t < HEADS:
                        mask_sp(t)
                    if 1 <= t <= HEADS:
                        mask_w(t - 1)

            pool.wait_ge(hi_done, 1)
            pool.wait_ge(h2T_psum, 2)
            link(nc.gpsimd.tensor_tensor(h2[:, 0, :], h2[:, 0, :], hbf[:, 0, 0, :], ALU.subtract))
            link(nc.gpsimd.tensor_copy(hbf[:, 1, 0, :], h2[:, 0, :]))
            nc.gpsimd.tensor_tensor(hbf[:, 2, 0, :], h2[:, 0, :], hbf[:, 1, 0, :], ALU.subtract)\
              .then_inc(split_done, 1)
            pool.wait_ge(mid_done, 1)
            nc.gpsimd.tensor_tensor(hbf[:, 2, 1, :], h2[:, 1, :], hbf[:, 1, 1, :], ALU.subtract)\
              .then_inc(split_done, 1)

            def pick_row(v, e):
                pool.wait_ge(up_done, v)
                nc.gpsimd.tensor_copy(rowsel[0:E, :], ident[0:E, bass.ds(e, 1)].to_broadcast([E, SLOTS]))\
                  .then_inc(bias_row, 1)

            nc.gpsimd.tensor_copy(rowsel[0:E, :], ident[0:E, 0:1].to_broadcast([E, SLOTS])).then_inc(bias_row, 1)
            with pool.Fori(1, E) as e:
                pick_row(e, e)
            pool.wait_ge(rounds_ready, 1)
            rounds = pool.value_load(rounds_i[0:1, 0:1], min_val=1, max_val=MAXR)
            with pool.If(rounds > 1):
                with pool.Fori(1, rounds) as r:
                    with pool.Fori(0, E) as e:
                        pick_row(r * E + e, e)

        @block.scalar
        def _(act):
            act.wait_ge(consts, 1)
            nc.scalar.activation(rsmall[:, 0:1], ident[:, 0:1], ACT.Sqrt)

            act.dma_start(par[:, 0, :], s5_lam_re[0].rearrange("(j g) p -> j (g p)", g=2)).then_inc(par_in, 16)
            act.dma_start(par[:, 1, :], s5_lam_im[0].rearrange("(j g) p -> j (g p)", g=2)).then_inc(par_in, 16)
            act.dma_start(par[:, 2, 0:2], s5_log_step[0].rearrange("(j g) -> j g", g=2)).then_inc(par_in, 16)
            act.dma_start(par[0:4, 15, :], s5_d[0].rearrange("(c g) h -> c (g h)", g=8)).then_inc(par_in, 16)

            def drain_h2T(a):
                act.wait_ge(h2T_psum, 2 * a + 1)
                nc.scalar.activation(hT[:, 0:4, a * P:(a + 1) * P],
                                     bank[2 + 2 * a][:, :].rearrange("p (c t) -> p c t", c=4), ACT.Copy)\
                 .then_inc(h2T_act, 1)

            nsq = [0]

            def squares(a, c):
                nsq[0] += 1
                if nsq[0] > 1:
                    act.wait_ge(sq_done, nsq[0] - 1)
                nc.scalar.activation(sq_junk, xres[:, a, c * 512:(c + 1) * 512], ACT.Square,
                                     accum_out=stat[:, 2 * a + c:2 * a + c + 1]).then_inc(sq_done, 1)

            def root(k):
                a = k % NT
                act.wait_ge(inv_done, k + 1)
                nc.scalar.activation(stat[:, 8 + a:9 + a], stat[:, 6 + a:7 + a], ACT.Sqrt).then_inc(rstd_done, 1)

            for a in range(NT):
                act.wait_ge(x_in[a], 16)
                for c in range(2):
                    squares(a, c)
            for a in range(NT):
                root(a)
            for b in range(2):
                act.wait_ge(hT_psum, b + 1)
                nc.scalar.activation(hT[:, 2 * b:2 * b + 2, :].rearrange("p c t -> p (c t)"),
                                     bank[b][:, :], ACT.Copy).then_inc(hT_act, 1)

            act.wait_ge(par_in, 64)
            nc.scalar.activation(par[:, 3, 0:2], par[:, 2, 0:2], ACT.Exp).then_inc(step_done, 1)
            act.wait_ge(arg_done, 1)
            nc.scalar.activation(par[:, 6, :], par[:, 4, :], ACT.Exp).then_inc(trig_done, 1)
            act.wait_ge(absa_done, 1)
            nc.scalar.activation(par[:, 8, :], par[:, 5, :], ACT.Sin).then_inc(trig_done, 1)
            nc.scalar.activation(par[:, 7, :], par[:, 9, :], ACT.Sin).then_inc(trig_done, 1)

            def drain_proj(n):
                g, half = GROUP_ORDER[n // 2], n % 2
                act.wait_ge(proj_done, n + 1)
                src = bank[n % 2][:, :]
                if g == 3:
                    dst, scale = uT[:, 2 * half:2 * half + 2, :].rearrange("p c t -> p (c t)"), 1.0
                elif g == 2:
                    dst, scale = vtok[:, half, :], 1.0
                elif g < 2:
                    c = 4 * g + 2 * half
                    dst, scale = qkT[:, c:c + 2, :].rearrange("p c t -> p (c t)"), (HD ** -0.5 if g == 0 else 1.0)
                else:
                    c = 4 * (g - 4) + 2 * half
                    if n == 8:
                        act.wait_ge(table_dve, 1)
                    dst, scale = gT[:, c:c + 2, :].rearrange("p c t -> p (c t)"), 1.0
                nc.scalar.activation(dst, src, ACT.Copy, scale=scale).then_inc(proj_read, 1)

            def soften(h):
                a = att[:, 0, h % 2, :]
                act.wait_ge(z_psum, h + 1)
                if h == 0:
                    act.wait_ge(table_pool, 1)
                if h >= 2:
                    act.wait_ge(sp_raw, h - 1)
                nc.scalar.activation(a, bank[2 + h % 2][:, 0:384], ACT.Abs).then_inc(absz_done, 1)
                act.wait_ge(absz_done, 3 * h + 1)
                nc.scalar.activation(a, a, ACT.Exp, scale=-1.0).then_inc(absz_done, 1)
                act.wait_ge(absz_done, 3 * h + 2)
                nc.scalar.activation(a, a, ACT.Ln, bias=1.0).then_inc(absz_done, 1)

            def weights(h):
                act.wait_ge(expo_psum, h + 1)
                if h >= 2:
                    act.wait_ge(ysb_psum, h - 1)
                nc.scalar.activation(att[:, 2, h % 2, :], bank[2 + h % 2][:, 0:384], ACT.Exp).then_inc(w_raw, 1)

            def drain_ysb(i):
                act.wait_ge(ysb_psum, 2 * i + 2)
                nc.scalar.activation(ysbT[:, i, :], bank[7][:, 0:T], ACT.Copy).then_inc(ysb_done, 1)

            def drain_tables():
                for i, (src, dst) in enumerate(((bank[4], BT[:, 0]), (bank[5], BT[:, 1]), (bank[7], CT[:, 0]),
                                                (bank[6], CT[:, 1]))):
                    act.wait_ge(bT_psum, i + 1)
                    nc.scalar.activation(dst.rearrange("p c n -> p (c n)"), src[:, :], ACT.Copy,
                                         scale=-1.0 if i == 3 else 1.0).then_inc(bT_done, 1)

            for u in range(UNITS):
                if u % 2 == 1:
                    drain_proj(u // 2)
                if u == BT_AFTER:
                    drain_tables()
                t = att_step(u)
                if t is not None:
                    if t == 4:
                        act.wait_ge(parT_psum, 1)
                    if t >= 4 and t % 2 == 0:
                        drain_ysb(t // 2 - 2)
                    if t < HEADS:
                        soften(t)
                    if 1 <= t <= HEADS:
                        weights(t - 1)
            drain_ysb(HEADS // 2 - 1)
            act.wait_ge(proj_read, NHALF)
            for i in range(2):
                nc.scalar.activation(gate_region[:, 2048 * i:2048 * (i + 1)],
                                     gate_region[:, 2048 * i:2048 * (i + 1)], ACT.Sigmoid).then_inc(gates_done, 1)
                act.wait_ge(gelu_arg, i + 1)
                nc.scalar.activation(gel[:, i, :], gel[:, i, :], ACT.Sigmoid, scale=GELU_S).then_inc(gelu_sig, 1)
            for i in range(2):
                act.wait_ge(glu_psum, i + 1)
                nc.scalar.activation(sgl[:, i, :], bank[i][:, :], ACT.Sigmoid).then_inc(glu_sig, 1)

            for i in range(4):
                act.wait_ge(x1_done, i + 1)
                squares(i // 2, i % 2)
                if i % 2 == 1:
                    root(NT + i // 2)
                if i == 2:
                    drain_h2T(0)
                    act.wait_ge(h2_done, 2)
                    nc.scalar.activation(hbf[:, 0, 0, :], h2[:, 0, :], ACT.Copy).then_inc(hi_done, 1)
            drain_h2T(1)
            act.wait_ge(h2_done, 4)
            nc.scalar.activation(hbf[:, 0, 1, :], h2[:, 1, :], ACT.Copy).then_inc(hi_done, 1)
            for a in range(NT):
                act.wait_ge(logit_sh, a + 1)
                nc.scalar.activation(rt[:, 2, a, :], rt[:, 5, a, :], ACT.Exp).then_inc(exp_done, 1)

            def drain_gather(v):
                act.wait_ge(gathered, v + 1)
                nc.scalar.activation(xT, bank[6][:, :], ACT.Copy).then_inc(xT_ready, 1)

            def expert(v):
                act.wait_ge(glu_ready, v + 1)
                nc.scalar.activation(sig, glu, ACT.Sigmoid, scale=ALPHA).then_inc(sig_ready, 1)
                drain_gather(v + 1)
                act.wait_ge(gsel_psum, v + 1)
                nc.scalar.activation(gsel.rearrange("p a t -> p (a t)"), bank[7][:, 0:T], ACT.Copy)\
                  .then_inc(gsel_ready, 1)

            drain_gather(0)
            act.wait_ge(gateT_psum, 1)
            nc.scalar.activation(gateT, bank[7][0:E, 0:T], ACT.Copy).then_inc(gateT_done, 1)
            with act.Fori(0, E) as v:
                expert(v)
            act.wait_ge(rounds_ready, 1)
            rounds = act.value_load(rounds_i[0:1, 0:1], min_val=1, max_val=MAXR)
            with act.If(rounds > 1):
                with act.Fori(1, rounds) as r:
                    with act.Fori(0, E) as e:
                        expert(r * E + e)

            nc.scalar.activation(rsmall[:, 0:1], ident[:, 0:1], ACT.Sqrt)
            for i in range(4):
                act.wait_ge(x1_done, 4 + i + 1)
                squares(i // 2, i % 2)
                if i % 2 == 1:
                    root(2 * NT + i // 2)

        @block.vector
        def _(dve):
            n = [0]

            def link(ins):
                n[0] += 1
                ins.then_inc(dve_step, 1)
                dve.wait_ge(dve_step, n[0])

            V = nc.vector

            def mean_square(k):
                a = k % NT
                dve.wait_ge(sq_done, 2 * (k + 1))
                link(V.tensor_tensor(stat[:, 4 + a:5 + a], stat[:, 2 * a:2 * a + 1],
                                     stat[:, 2 * a + 1:2 * a + 2], ALU.add))
                link(V.tensor_scalar(stat[:, 4 + a:5 + a], stat[:, 4 + a:5 + a], 1.0 / D, EPS,
                                     ALU.mult, ALU.add))
                V.reciprocal(stat[:, 6 + a:7 + a], stat[:, 4 + a:5 + a]).then_inc(inv_done, 1)

            def scale(k, dst, done, parts=1):
                a, w = k % NT, D // parts
                dve.wait_ge(rstd_done, k + 1)
                dve.wait_ge(gain_in, 16 * (k // NT + 1))
                for c in range(parts):
                    n = slice(c * w, (c + 1) * w)
                    V.scalar_tensor_tensor(dst[:, a, n], xres[:, a, n], stat[:, 8 + a:9 + a], gain[:, n],
                                           ALU.mult, ALU.mult).then_inc(done, 1)

            for a in range(NT):
                mean_square(a)
            for a in range(NT):
                scale(a, xn, xn_done)
            for b in (2, 3):
                dve.wait_ge(hT_psum, b + 1)
                V.tensor_copy(hT[:, 2 * b:2 * b + 2, :].rearrange("p c t -> p (c t)"), bank[b][:, :])\
                 .then_inc(hT_dve, 1)

            step = par[:, 3, 0:2].unsqueeze(2).to_broadcast([PAIRS, 2, NSTATE])

            def pv(i):
                return par[:, i, :].rearrange("p (g n) -> p g n", g=2)

            dve.wait_ge(step_done, 1)
            V.tensor_tensor(pv(4), pv(0), step, ALU.mult).then_inc(arg_done, 1)
            link(V.tensor_tensor(pv(5), pv(1), step, ALU.mult))
            link(V.tensor_scalar(par[:, 10, :], par[:, 5, :], 1.0 / TWO_PI, None, ALU.mult))
            link(V.tensor_scalar(par[:, 10, :], par[:, 10, :], MAGIC, None, ALU.add))
            link(V.tensor_scalar(par[:, 10, :], par[:, 10, :], MAGIC, None, ALU.subtract))
            for part in (PI_A, PI_B, PI_C):
                link(V.scalar_tensor_tensor(par[:, 5, :], par[:, 10, :], -part, par[:, 5, :],
                                            ALU.mult, ALU.add))
            link(V.tensor_scalar(par[:, 5, :], par[:, 5, :], 3.1415925, -3.1415925, ALU.min, ALU.max))
            link(V.scalar_tensor_tensor(par[:, 9, :], par[:, 5, :], -1.0, par[:, 5, :], ALU.mult, ALU.max))
            V.tensor_scalar(par[:, 9, :], par[:, 9, :], -1.0, TWO_PI / 4, ALU.mult, ALU.add)\
             .then_inc(absa_done, 1)

            dve.wait_ge(trig_done, 3)
            link(V.tensor_tensor(par[:, 10, :], par[:, 6, :], par[:, 7, :], ALU.mult))
            link(V.tensor_scalar(par[:, 10, :], par[:, 10, :], 1.0, None, ALU.subtract))
            link(V.tensor_tensor(par[:, 11, :], par[:, 6, :], par[:, 8, :], ALU.mult))
            link(V.tensor_tensor(par[:, 12, :], par[:, 0, :], par[:, 0, :], ALU.mult))
            link(V.tensor_tensor(par[:, 13, :], par[:, 1, :], par[:, 1, :], ALU.mult))
            link(V.tensor_tensor(par[:, 12, :], par[:, 12, :], par[:, 13, :], ALU.add))
            link(V.reciprocal(par[:, 12, :], par[:, 12, :]))
            link(V.tensor_tensor(par[:, 13, :], par[:, 10, :], par[:, 0, :], ALU.mult))
            link(V.tensor_tensor(par[:, 14, :], par[:, 11, :], par[:, 1, :], ALU.mult))
            link(V.tensor_tensor(par[:, 13, :], par[:, 13, :], par[:, 14, :], ALU.add))
            link(V.tensor_tensor(par[:, 9, :], par[:, 13, :], par[:, 12, :], ALU.mult))
            link(V.tensor_tensor(par[:, 13, :], par[:, 11, :], par[:, 0, :], ALU.mult))
            link(V.tensor_tensor(par[:, 14, :], par[:, 10, :], par[:, 1, :], ALU.mult))
            link(V.tensor_tensor(par[:, 13, :], par[:, 13, :], par[:, 14, :], ALU.subtract))
            V.tensor_tensor(par[:, 10, :], par[:, 13, :], par[:, 12, :], ALU.mult).then_inc(par_done, 1)
            dve.wait_ge(par_done, 1)
            dve.wait_ge(parT_psum, 1)
            V.tensor_copy(parT[:, :, :].rearrange("p i j -> p (i j)"), bank[6][:, 0:5 * PAIRS])\
             .then_inc(parT_done, 1)
            V.tensor_copy(dcol[:, :], bank[6][:, 5 * PAIRS:5 * PAIRS + 4]).then_inc(parT_done, 1)
            dve.wait_ge(parT_done, 2)
            V.tensor_copy(cosT[:, :, 0:1], parT[:, 1, :].unsqueeze(2)).then_inc(seed_done, 1)
            V.tensor_copy(sinT[:, :, 0:1], parT[:, 2, :].unsqueeze(2)).then_inc(seed_done, 1)

            dve.wait_ge(idx_ready, 1)
            link(V.tensor_scalar(pidx[:, 1:2], pidx[:, 0:1], 6, 1, ALU.arith_shift_right, ALU.bitwise_and))
            link(V.tensor_scalar(pidx[:, 2:3], pidx[:, 0:1], 4, 1, ALU.arith_shift_right, ALU.bitwise_and))
            link(V.tensor_copy(gmask[:, 1:4:2], pidx[:, 1:3]))
            link(V.tensor_scalar(gmask[:, 0:3:2], gmask[:, 1:4:2], -1.0, 1.0, ALU.mult, ALU.add))

            dve.wait_ge(bc_in, 64)
            f = [parT[:, 3 + r, :].unsqueeze(2).to_broadcast([P, PAIRS, GCH]) for r in range(2)]
            link(V.tensor_tensor(b_bar[:, 0], b_raw[:, 0], f[0], ALU.mult))
            link(V.tensor_tensor(b_tmp[:, 0], b_raw[:, 1], f[1], ALU.mult))
            link(V.tensor_tensor(b_bar[:, 0], b_bar[:, 0], b_tmp[:, 0], ALU.subtract))
            link(V.tensor_tensor(b_bar[:, 1], b_raw[:, 1], f[0], ALU.mult))
            link(V.tensor_tensor(b_tmp[:, 1], b_raw[:, 0], f[1], ALU.mult))
            link(V.tensor_tensor(b_bar[:, 1], b_bar[:, 1], b_tmp[:, 1], ALU.add))
            for r in range(2):
                for g in range(2):
                    V.tensor_scalar(b_pad[:, r, :, g, :], b_bar[:, r], gmask[:, g:g + 1], None, ALU.mult)\
                     .then_inc(bpad_done, 1)
            for r in range(2):
                for g in range(2):
                    V.tensor_scalar(c_pad[:, r, :, g, :], c_raw[:, r], gmask[:, 2 + g:3 + g], None, ALU.mult)\
                     .then_inc(bpad_done, 1)
            dve.wait_ge(seed_done, 2)
            dve.wait_ge(xn_done, NT)
            build_table(V, link, slice(0, PAIRS // 2), tab_dve)
            V.memset(stat[:, 10:11], 0.0).then_inc(table_dve, 1)

            def two(ap):
                return ap.rearrange("p (r t) -> p r t", r=2)

            def rotate_in(j):
                b = j % 2
                if j == PAIRS // 2:
                    dve.wait_ge(table_pool, 1)
                dve.wait_ge(bu_done, 2 * (j + 1))
                if j >= 2:
                    dve.wait_ge(mrot_done, 2 * (j - 1))
                for i, table in enumerate((cosT, sinT)):
                    V.tensor_tensor(two(s5b[:, i, b, :]), two(bank[4 + b][:, :]),
                                    table[:, j:j + 1, :].to_broadcast([P, 2, T]), ALU.mult)\
                     .then_inc(bu_read, 1)

            def scan(j):
                b = j % 2
                m, sc = s5b[:, 2, b, :], s5b[:, 3, b, :]
                mag = parT[:, 0, j:j + 1].to_broadcast([P, T])
                dve.wait_ge(mrot_done, 2 * (j + 1))
                if j >= 2:
                    dve.wait_ge(psin_done, j - 1)
                    dve.wait_ge(ys5_psum, j - 1)
                for r in range(2):
                    V.tensor_tensor_scan(sc[:, r * T:(r + 1) * T], mag, m[:, r * T:(r + 1) * T], 0.0,
                                         ALU.mult, ALU.add).then_inc(scan_done, 1)
                dve.wait_ge(scan_done, 2 * (j + 1))
                V.tensor_tensor(two(s5b[:, 4, b, :]), two(sc),
                                cosT[:, j:j + 1, :].to_broadcast([P, 2, T]), ALU.mult).then_inc(pcos_done, 1)

            def state(j):
                p1, p2 = s5b[:, 4, j % 2, :], s5b[:, 5, j % 2, :]
                dve.wait_ge(psin_done, j + 1)
                dve.wait_ge(pcos_done, j + 1)
                V.tensor_tensor(p1[:, 0:T], p1[:, 0:T], p2[:, T:2 * T], ALU.subtract).then_inc(state_done, 1)
                V.tensor_tensor(p1[:, T:2 * T], p1[:, T:2 * T], p2[:, 0:T], ALU.add).then_inc(state_done, 1)

            def softplus(h):
                dve.wait_ge(absz_done, 3 * (h + 1))
                if h >= 2:
                    dve.wait_ge(expo_psum, h - 1)
                V.scalar_tensor_tensor(att[:, 1, h % 2, :], bank[2 + h % 2][:, 0:384], 0.0,
                                       att[:, 0, h % 2, :], ALU.max, ALU.add).then_inc(sp_raw, 1)

            def drain_s5(c):
                dve.wait_ge(ys5_psum, CW * (c + 1))
                V.scalar_tensor_tensor(ygT[:, c, :], uT[:, c, :], dcol[:, c:c + 1],
                                       bank[6][:, 0:T], ALU.mult, ALU.add)\
                 .then_inc(ys5_read, 1)

            for u in range(UNITS):
                s = s5_step(u)
                if s is not None:
                    if s >= 6 and (s - 6) % CW == 0:
                        drain_s5((s - 6) // CW)
                    if s >= 2:
                        state(s - 2)
                    if s < PAIRS:
                        rotate_in(s)
                    if 1 <= s <= PAIRS:
                        scan(s - 1)
                t = att_step(u)
                if t is not None and t < HEADS:
                    softplus(t)
            drain_s5(3)

            dve.wait_ge(ys5_read, 4)
            for i in range(2):
                y = ygT[:, 2 * i:2 * i + 2, :].rearrange("p c t -> p (c t)")
                link(V.tensor_tensor(gel[:, i, :], y, y, ALU.mult))
                link(V.tensor_scalar(gel[:, i, :], gel[:, i, :], GELU_C, 1.0, ALU.mult, ALU.add))
                V.tensor_tensor(gel[:, i, :], gel[:, i, :], y, ALU.mult).then_inc(gelu_arg, 1)
            for i in range(2):
                y = ygT[:, 2 * i:2 * i + 2, :].rearrange("p c t -> p (c t)")
                dve.wait_ge(gelu_sig, i + 1)
                V.tensor_tensor(y, y, gel[:, i, :], ALU.mult).then_inc(yg_done, 1)

            def open_merge(q):
                dve.wait_ge(gates_done, 1)
                dve.wait_ge(br_psum, q + 1)
                V.tensor_tensor(hT[:, 2 * q:2 * q + 2, :].rearrange("p c t -> p (c t)"), bank[2 + q][:, :],
                                gT[:, 2 * q:2 * q + 2, :].rearrange("p c t -> p (c t)"), ALU.mult)\
                 .then_inc(merged_sb, 1)

            for q in range(2):
                open_merge(q)
            for i in range(2):
                dve.wait_ge(glu_sig, i + 1)
                V.tensor_tensor(ys5T[:, 2 * i:2 * i + 2, :].rearrange("p c t -> p (c t)"),
                                ygT[:, 2 * i:2 * i + 2, :].rearrange("p c t -> p (c t)"),
                                sgl[:, i, :], ALU.mult).then_inc(ys5_done, 1)
            for q in (2, 3):
                open_merge(q)

            dve.wait_ge(gates_done, 2)
            dve.wait_ge(merged_sb, 4)
            for q in range(4):
                dve.wait_ge(br_psum, 5 + q)
                link(V.tensor_tensor(mrg[:, q % 2, :], bank[2 + q][:, :],
                                     gT[:, 8 + 2 * q:10 + 2 * q, :].rearrange("p c t -> p (c t)"), ALU.mult))
                h = hT[:, 2 * q:2 * q + 2, :].rearrange("p c t -> p (c t)")
                V.tensor_tensor(h, h, mrg[:, q % 2, :], ALU.add).then_inc(merged, 1)

            def drain_h2T(a):
                dve.wait_ge(h2T_psum, 2 * a + 2)
                V.tensor_copy(hT[:, 4:8, a * P:(a + 1) * P],
                              bank[3 + 2 * a][:, :].rearrange("p (c t) -> p c t", c=4)).then_inc(h2T_dve, 1)

            lg, mk, ex, gt, rk, scr = (rt[:, i] for i in range(6))
            dve.wait_ge(rw_in, 32)
            dve.wait_ge(consts, 7)

            def route(a):
                dve.wait_ge(logit_psum, a + 1)
                link(V.tensor_tensor(lg[:, a, :], bank[0 + a][:, 0:E], br[:, :], ALU.add))
                link(V.max(rtop[:, a, :], lg[:, a, :]))
                V.tensor_scalar(scr[:, a, :], lg[:, a, :], rtop[:, a, 0:1], None, ALU.subtract)\
                 .then_inc(logit_sh, 1)
                link(V.max_index(ridx[:, a, :], rtop[:, a, :], lg[:, a, :]))
                link(V.tensor_copy(ridxf[:, a, :], ridx[:, a, :]))
                link(V.tensor_tensor(hits[:, a], iota_e[:, :].unsqueeze(1).to_broadcast([P, TOPK, E]),
                                     ridxf[:, a, 0:TOPK].unsqueeze(2).to_broadcast([P, TOPK, E]), ALU.is_equal))
                link(V.tensor_reduce(mk[:, a, :], hits[:, a].rearrange("p k e -> p e k"), AX.X, ALU.add))
                V.tensor_copy(mask_bf[:, a, :], mk[:, a, :]).then_inc(mask_done, 1)

            for i in range(4):
                a, c = i // 2, i % 2
                dve.wait_ge(mix_psum, i + 1)
                V.tensor_tensor(xres[:, a, c * 512:(c + 1) * 512], xres[:, a, c * 512:(c + 1) * 512],
                                bank[MB[i]][:, :], ALU.add).then_inc(x1_done, 1)
                if i % 2 == 1:
                    mean_square(NT + a)
                    scale(NT + a, h2, h2_done, parts=2)
                if i == 2:
                    drain_h2T(0)
            drain_h2T(1)
            route(0)
            dve.wait_ge(hi_done, 2)
            dve.wait_ge(h2T_psum, 4)
            link(V.tensor_tensor(h2[:, 1, :], h2[:, 1, :], hbf[:, 0, 1, :], ALU.subtract))
            V.tensor_copy(hbf[:, 1, 1, :], h2[:, 1, :]).then_inc(mid_done, 1)
            route(1)

            link(V.tensor_scalar(rk, mk, -NOT_ROUTED, NOT_ROUTED, ALU.mult, ALU.add))
            dve.wait_ge(rank_psum, 1)
            link(V.tensor_tensor(rk, rk, bank[5][:, 0:NT * E].rearrange("p (a e) -> p a e", a=NT), ALU.add))
            link(V.reduce_max(rsmall[:, 5:6], bank[5][:, NT * E:NT * E + E], AX.X))
            for a in range(NT):
                V.tensor_scalar(ponehot[:, a, :], iota_s[:, 0:SLOTS], rk[:, a, 0:1], None,
                                ALU.is_equal).then_inc(onehot_ready, 1)

            for a in range(NT):
                dve.wait_ge(exp_done, a + 1)
            link(V.tensor_tensor(ex, ex, mk, ALU.mult))
            link(V.tensor_reduce(rsmall[:, 1:3], ex, AX.X, ALU.add))
            link(V.reciprocal(rsmall[:, 3:5], rsmall[:, 1:3]))
            V.tensor_tensor(gt, ex, rsmall[:, 3:5].unsqueeze(2).to_broadcast([P, NT, E]), ALU.mult)\
             .then_inc(gates_ready, 1)
            dve.wait_ge(gates_ready, 1)
            for r in range(MAXR + 1):
                w = min(E, NV - r * E)
                link(V.tensor_scalar(rank_x[:, :, r * E:r * E + w], rk[:, :, 0:w], float(r * SLOTS), None,
                                     ALU.subtract))
                link(V.tensor_copy(gate_x[:, :, r * E:r * E + w], gt[:, :, 0:w]))

            def one_hot(v):
                dve.wait_ge(gathered, v)
                for a in range(NT):
                    V.tensor_scalar(ponehot[:, a, :], iota_s[:, 0:SLOTS], rank_x[:, a, bass.ds(v, 1)], None,
                                    ALU.is_equal).then_inc(onehot_ready, 1)

            link(V.tensor_scalar(rsmall[:, 6:7], rsmall[:, 5:6], float(SLOTS), 1.0, ALU.is_gt, ALU.add))
            for r in range(2, MAXR):
                link(V.scalar_tensor_tensor(rsmall[:, 6:7], rsmall[:, 5:6], float(r * SLOTS), rsmall[:, 6:7],
                                            ALU.is_gt, ALU.add))
            V.tensor_copy(rounds_i[:, :], rsmall[:, 6:7]).then_inc(rounds_ready, 1)

            def expert(v):
                for a in range(NT):
                    V.tensor_scalar(pgate[:, a, :], iota_s[:, :], rank_x[:, a, bass.ds(v, 1)],
                                    gate_x[:, a, bass.ds(v, 1)], ALU.is_equal, ALU.mult)\
                     .then_inc(pgate_ready, 1)
                one_hot(v + 1)
                dve.wait_ge(up_done, v + 1)
                V.tensor_scalar(glu, bank[4][:, :], LIMIT, None, ALU.min).then_inc(glu_ready, 1)
                V.tensor_scalar(lin, bank[5][:, :], LIMIT, -LIMIT, ALU.min, ALU.max).then_inc(lin_ready, 1)
                dve.wait_ge(sig_ready, v + 1)
                dve.wait_ge(glu_ready, v + 1)
                V.tensor_tensor(glu, glu, sig, ALU.mult).then_inc(prod_ready, 1)
                dve.wait_ge(lin_ready, v + 1)
                dve.wait_ge(prod_ready, v + 1)
                V.scalar_tensor_tensor(actv, lin, 1.0, glu, ALU.add, ALU.mult).then_inc(act_ready, 1)
                dve.wait_ge(actT_psum, v + 1)
                V.tensor_copy(actT, bank[6][:, :]).then_inc(actT_ready, 1)
                dve.wait_ge(chunk_used, v * RING + RING)
                V.tensor_copy(yslot, bank[7][:, :]).then_inc(y_ready, 1)

            with dve.Fori(0, E) as v:
                expert(v)
            dve.wait_ge(rounds_ready, 1)
            rounds = dve.value_load(rounds_i[0:1, 0:1], min_val=1, max_val=MAXR)
            with dve.If(rounds > 1):
                with dve.Fori(1, rounds) as r:
                    with dve.Fori(0, E) as e:
                        expert(r * E + e)

            def add_moe(i):
                a, c = i // 2, i % 2
                dve.wait_ge(mix_psum, 4 + i + 1)
                V.tensor_tensor(xres[:, a, c * 512:(c + 1) * 512], xres[:, a, c * 512:(c + 1) * 512],
                                bank[i][:, :], ALU.add).then_inc(x1_done, 1)

            for i in range(3):
                add_moe(i)
            mean_square(2 * NT)
            add_moe(3)
            scale(2 * NT, xres, out_done, parts=2)
            mean_square(2 * NT + 1)
            scale(2 * NT + 1, xres, out_done, parts=2)

        @block.tensor
        def _(pe):
            M = nc.tensor

            pe.wait_ge(consts, 1)
            for b in range(4):
                for kc in (2 * b, 2 * b + 1):
                    for a in range(NT):
                        pe.wait_ge(xn_done, a + 1)
                        last = M.transpose(bank[b][:, (kc % 2) * T + a * P:(kc % 2) * T + (a + 1) * P],
                                           xn[:, a, kc * P:(kc + 1) * P], ident[:, :])
                last.then_inc(hT_psum, 1)
            def small_parameters():
                pe.wait_ge(par_done, 1)
                for i in range(5):
                    M.transpose(bank[6][:, i * PAIRS:(i + 1) * PAIRS], par[:, 6 + i, :],
                                ident[0:PAIRS, 0:PAIRS])
                M.transpose(bank[6][:, 5 * PAIRS:5 * PAIRS + 4], par[0:4, 15, :], ident[0:4, 0:4])\
                 .then_inc(parT_psum, 1)

            def project(u):
                n, sub = u // 2, u % 2
                i, half = n // 2, n % 2
                g, w = GROUP_ORDER[i], win(i % WIN_SLOTS)
                if half == 0 and sub == 0:
                    pe.wait_ge(win_in[i % WIN_SLOTS], 16 * (i // WIN_SLOTS + 1))
                if u == 2:
                    pe.wait_ge(win_half, 16)
                if n >= 2 and sub == 0:
                    pe.wait_ge(proj_read, n - 1)
                o = bank[n % 2]
                if g == 2:
                    for kc in range(4 * sub, 4 * sub + 4):
                        last = M.matmul(o[:, :], hT[:, kc, half * P:(half + 1) * P], w[:, kc, :],
                                        start=(kc == 0), stop=(kc == KC - 1))
                else:
                    m = 2 * half + sub
                    for kc in range(KC):
                        last = M.matmul(o[:, sub * T:(sub + 1) * T], w[:, kc, m * P:(m + 1) * P], hT[:, kc, :],
                                        start=(kc == 0), stop=(kc == KC - 1))
                if sub == 1:
                    last.then_inc(proj_done, 1)

            def bu(j):
                c, r0 = j // CW, 32 * (j % CW)
                if j >= 2:
                    pe.wait_ge(bu_read, 2 * (j - 1))
                for r in range(2):
                    M.matmul(bank[4 + j % 2][:, r * T:(r + 1) * T], BT[r0:r0 + 32, r, c, :],
                             uT[r0:r0 + 32, c, :], start=True, stop=True).then_inc(bu_done, 1)

            def s5_out(j):
                c, r0, b = j // CW, 32 * (j % CW), j % 2
                pe.wait_ge(state_done, 2 * (j + 1))
                if c >= 1 and j % CW == 0:
                    pe.wait_ge(ys5_read, c)
                o = bank[6][r0:r0 + 32, 0:T]
                for i in range(2):
                    last = M.matmul(o, CT[:, i, c, r0:r0 + 32], s5b[:, 4, b, i * T:(i + 1) * T],
                                    start=(i == 0), stop=(i == 1))
                last.then_inc(ys5_psum, 1)

            def scores(h):
                r0, c = HD * (h % 2), h // 2
                q, k = qkT[r0:r0 + HD, c, :], qkT[r0:r0 + HD, 4 + c, :]
                if h >= 2:
                    pe.wait_ge(w_raw, h - 1)
                z = bank[2 + h % 2]
                M.matmul(z[:, 0:T], k[:, 0:P], q, start=True, stop=True)
                M.matmul(z[:, T:T + P], k[:, P:T], q[:, P:T], start=False, stop=True, skip_group_check=True)\
                 .then_inc(z_psum, 1)

            def exponents(h):
                pe.wait_ge(sp_done, h + 1)
                z, spt = bank[2 + h % 2], att[:, 1, h % 2, :]
                M.matmul(z[:, 0:T], neg_tri[:, :], spt[:, 0:T], start=False, stop=True,
                         skip_group_check=True)
                M.matmul(z[:, P:T], neg_ones[:, :], spt[:, T:T + P], start=False, stop=True,
                         skip_group_check=True)
                M.matmul(z[:, T:T + P], neg_tri[:, :], spt[:, T:T + P], start=False, stop=True,
                         skip_group_check=True)\
                 .then_inc(expo_psum, 1)

            def attend(h):
                r0, i = HD * (h % 2), h // 2
                pe.wait_ge(w_done, h + 1)
                if h >= 2 and h % 2 == 0:
                    pe.wait_ge(ysb_done, i)
                w = att[:, 2, h % 2, :]
                o = bank[7][r0:r0 + HD, 0:T]
                M.matmul(o, vtok[:, 0, h * HD:(h + 1) * HD], w[:, 0:T], start=True, stop=False)
                M.matmul(o[:, P:T], vtok[:, 1, h * HD:(h + 1) * HD], w[:, T:T + P], start=False, stop=True)\
                 .then_inc(ysb_psum, 1)

            pe.wait_ge(hT_act, 2)
            pe.wait_ge(hT_dve, 2)
            project(0)
            project(1)
            project(2)
            small_parameters()
            for u in range(3, BT_AFTER + 1):
                project(u)
            for r in range(2):
                pe.wait_ge(bpad_done, 2 * (r + 1))
                for c in range(4):
                    last = M.transpose(bank[4 + r][:, c * P:(c + 1) * P],
                                       b_pad[:, r, CW * c:CW * (c + 1)].rearrange("p j g h -> p (j g h)"),
                                       ident[:, :])
                last.then_inc(bT_psum, 1)
            pe.wait_ge(parT_done, 2)
            for r in range(2):
                pe.wait_ge(bpad_done, 4 + 2 * (r + 1))
                for c in range(4):
                    last = M.transpose(bank[7 - r][:, c * P:(c + 1) * P],
                                       c_pad[:, r, c].rearrange("p g n -> p (g n)"), ident[:, :])
                last.then_inc(bT_psum, 1)
            for u in range(BT_AFTER + 1, UNITS):
                project(u)
                s = s5_step(u)
                if s is not None:
                    if s == 0:
                        pe.wait_ge(bT_done, 4)
                        pe.wait_ge(proj_read, 2)
                    if s < PAIRS:
                        bu(s)
                    if s >= 2:
                        s5_out(s - 2)
                t = att_step(u)
                if t is not None:
                    if t == 0:
                        pe.wait_ge(consts, 3)
                        pe.wait_ge(proj_read, 6)
                    if t == 2:
                        pe.wait_ge(proj_read, 8)
                    if t < HEADS:
                        scores(t)
                    if 1 <= t <= HEADS:
                        exponents(t - 1)
                    if t >= 2:
                        attend(t - 2)

            def branch(q, w, y, last_chunk=None):
                for c in range(2):
                    m = 2 * q + c
                    for kc in range(4):
                        if q == 0 and c == 0 and kc == 3 and last_chunk is not None:
                            pe.wait_ge(last_chunk, HEADS // 2)
                        last = M.matmul(bank[2 + q][:, c * T:(c + 1) * T], w[:, kc, m * P:(m + 1) * P],
                                        y[:, kc, :], start=(kc == 0), stop=(kc == 3))
                last.then_inc(br_psum, 1)

            pe.wait_ge(mixw_in[1], 16)
            pe.wait_ge(ysb_done, HEADS // 2 - 1)
            pe.wait_ge(w_raw, HEADS)
            pe.wait_ge(bu_read, 2 * PAIRS)
            for q in range(2):
                branch(q, sb_w, ysbT, ysb_done)

            pe.wait_ge(mixw_in[0], 16)
            pe.wait_ge(yg_done, 2)
            pe.wait_ge(proj_read, NHALF)
            for i in range(2):
                for c in range(2):
                    m = 2 * i + c
                    for kc in range(4):
                        last = M.matmul(bank[i][:, c * T:(c + 1) * T], glu_w[:, kc, m * P:(m + 1) * P],
                                        ygT[:, kc, :], start=(kc == 0), stop=(kc == 3))
                last.then_inc(glu_psum, 1)

            for q in (2, 3):
                branch(q, sb_w, ysbT)

            pe.wait_ge(mixw_in[2], 16)
            pe.wait_ge(ys5_done, 2)
            for q in range(4):
                pe.wait_ge(merged_sb, q + 1)
                branch(q, s5_w, ys5T)

            def mix_out(i):
                a, c = i // 2, i % 2
                for kc in range(KC):
                    pe.wait_ge(merged, kc // 2 + 1)
                    last = M.matmul(bank[MB[i]][:, :], hT[:, kc, a * P:(a + 1) * P],
                                    out_w[:, kc, c * 512:(c + 1) * 512], start=(kc == 0), stop=(kc == KC - 1))
                last.then_inc(mix_psum, 1)

            def turn_h2(a):
                for b in range(2):
                    pe.wait_ge(h2_done, 2 * a + b + 1)
                    for c in range(4):
                        last = M.transpose(bank[2 + 2 * a + b][:, c * P:(c + 1) * P],
                                           h2[:, a, (4 * b + c) * P:(4 * b + c + 1) * P], ident[:, :])
                    last.then_inc(h2T_psum, 1)

            def logits(a):
                pe.wait_ge(h2T_act, a + 1)
                pe.wait_ge(h2T_dve, a + 1)
                for kc in range(KC):
                    last = M.matmul(bank[a][:, 0:E], hT[:, kc, a * P:(a + 1) * P], wr[:, kc, :],
                                    start=(kc == 0), stop=(kc == KC - 1))
                last.then_inc(logit_psum, 1)

            pe.wait_ge(mixw_in[3], 16)
            pe.wait_ge(ys5_read, 4)
            for i in range(3):
                mix_out(i)
            turn_h2(0)
            mix_out(3)
            pe.wait_ge(rw_in, 32)
            logits(0)
            turn_h2(1)
            logits(1)
            pe.wait_ge(mask_done, NT)
            pe.wait_ge(consts, 5)
            M.matmul(bank[5][:, 0:E], tri_bf[:, :], mask_bf[:, 0, :], start=True, stop=True)
            M.matmul(bank[5][:, E:2 * E], ones_bf[:, :], mask_bf[:, 0, :], start=True, stop=False)
            M.matmul(bank[5][:, E:2 * E], tri_bf[:, :], mask_bf[:, 1, :], start=False, stop=True)
            M.matmul(bank[5][:, 2 * E:3 * E], ones_bf[:, :], mask_bf[:, 0, :], start=True, stop=False)
            M.matmul(bank[5][:, 2 * E:3 * E], ones_bf[:, :], mask_bf[:, 1, :], start=False, stop=True)\
             .then_inc(rank_psum, 1)

            def gather(v):
                pe.wait_ge(onehot_ready, (v + 1) * NT)
                for kc in range(KC):
                    k = 0
                    for i in range(3):
                        for a in range(NT):
                            last = M.matmul(bank[6][:, kc * SLOTS:(kc + 1) * SLOTS],
                                            hbf[:, i, a, kc * P:(kc + 1) * P], ponehot[:, a, :],
                                            start=(k == 0), stop=(k == 3 * NT - 1))
                            k += 1
                last.then_inc(gathered, 1)

            def scatter(v, last=False):
                pe.wait_ge(y_ready, v)
                for a in range(NT):
                    for c in range(2):
                        r = slice(SLOTS * c, SLOTS * (c + 1))
                        ins = M.matmul(bank[2 * a + c][:, :], gsel[r, a, :], yslot[r, :],
                                       start=False, stop=last)
                        if last:
                            ins.then_inc(mix_psum, 1)

            def open_output():
                pe.wait_ge(gateT_done, 1)
                pe.wait_ge(bias_in, 32)
                for a in range(NT):
                    for c in range(2):
                        M.matmul(bank[2 * a + c][:, :], gateT[:, a * P:(a + 1) * P],
                                 bdn[:, c * 512:(c + 1) * 512], start=True, stop=False)

            def expert(v, first=False):
                pe.wait_ge(xT_ready, v + 1)
                for k in range(UPC):
                    if k == 2 and not first:
                        scatter(v)
                    pe.wait_ge(chunk_in[k], (v + 1) * 16)
                    for q in range(4):
                        r = SLOTS * (q % 2)
                        last = M.matmul(bank[4 + q // 2][r:r + SLOTS, :], xT[:, k * SLOTS:(k + 1) * SLOTS],
                                        ring[:, k, q * 512:(q + 1) * 512], start=(k == 0), stop=False)
                    last.then_inc(chunk_used, 1)
                pe.wait_ge(bias_row, v + 1)
                for q in range(4):
                    r = SLOTS * (q % 2)
                    last = M.matmul(bank[4 + q // 2][r:r + SLOTS, :], rowsel[0:E, :],
                                    bup[:, q * 512:(q + 1) * 512], start=False, stop=True)
                last.then_inc(up_done, 1)
                if first:
                    open_output()
                gather(v + 1)
                pe.wait_ge(pgate_ready, (v + 1) * NT)
                for a in range(NT):
                    last = M.transpose(bank[7][:, a * P:(a + 1) * P], pgate[:, a, :], ident[:, :])
                last.then_inc(gsel_psum, 1)
                pe.wait_ge(act_ready, v + 1)
                pe.wait_ge(xT_ready, v + 2)
                for j in range(4):
                    last = M.transpose(bank[6][:, j * P:(j + 1) * P], actv[:, j * P:(j + 1) * P], ident[:, :])
                last.then_inc(actT_psum, 1)
                pe.wait_ge(actT_ready, v + 1)
                pe.wait_ge(gsel_ready, v + 1)
                for k in range(KC):
                    if k % 2 == 0:
                        pe.wait_ge(chunk_in[UPC + k // 2], (v + 1) * 16)
                    f = (k % 4) * P + (k // 4) * SLOTS
                    for c in range(2):
                        r, n0 = SLOTS * c, (k % 2) * D + c * 512
                        last = M.matmul(bank[7][r:r + SLOTS, :], actT[:, f:f + SLOTS],
                                        ring[:, UPC + k // 2, n0:n0 + 512], start=(k == 0), stop=(k == KC - 1))
                    if k % 2 == 1:
                        last.then_inc(chunk_used, 1)

            pe.wait_ge(split_done, NT)
            gather(0)
            pe.wait_ge(gates_ready, 1)
            for a in range(NT):
                last = M.transpose(bank[7][0:E, a * P:(a + 1) * P], rt[:, 3, a, :], ident[:, :])
            last.then_inc(gateT_psum, 1)
            expert(0, first=True)
            with pe.Fori(1, E) as v:
                expert(v)
            pe.wait_ge(rounds_ready, 1)
            rounds = pe.value_load(rounds_i[0:1, 0:1], min_val=1, max_val=MAXR)
            with pe.If(rounds > 1):
                with pe.Fori(1, rounds) as r:
                    with pe.Fori(0, E) as e:
                        expert(r * E + e)
            scatter(rounds * E, last=True)


_INS = ['x', 'norm_mix', 'w_in', 's5_lam_re', 's5_lam_im', 's5_b_re', 's5_b_im', 's5_c_re', 's5_c_im',
        's5_d', 's5_log_step', 'w_glu', 'w_branch_sb', 'w_branch_s5', 'w_out', 'norm_ffn', 'w_router',
        'b_router', 'w_up', 'b_up', 'w_down', 'b_down', 'norm_final']


def kernel(**inputs):
    import numpy as np
    import concourse.bacc as bacc
    from concourse.bass_utils import run_bass_kernel_spmd

    nc = bacc.Bacc("TRN2", target_bir_lowering=False, num_devices=1)
    arrays, args = {}, []
    for name in _INS:
        a = np.ascontiguousarray(inputs[name])
        arrays[f"in_{name}"] = a
        args.append(nc.dram_tensor(f"in_{name}", a.shape, mybir.dt.from_np(a.dtype), kind="ExternalInput").ap())
    out = nc.dram_tensor("out", (1, T, D), F32, kind="ExternalOutput").ap()
    build(nc, *args, out)
    r = run_bass_kernel_spmd(nc, [arrays], core_ids=[0])
    return r.results[0]["out"]
```
